# Optimizing a Trainium2 kernel written in Bass

```python
import math
import jax, jax.numpy as jnp
from jax import lax
import numpy as np

D_MODEL = 1024
BATCH = 1
SEQ = 256
DEPTH = 1

N_HEADS = 8
HEAD_DIM = 64
ATTN_WIDTH = N_HEADS * HEAD_DIM
ATTN_SCALE = HEAD_DIM ** -0.5
IDX_HEADS = 8
IDX_DIM = 64
IDX_SCALE = (IDX_HEADS ** -0.5) * (IDX_DIM ** -0.5)
TOPK_MAX = 256
Q_BLOCK = 128
CONV_CH = 512
CONV_WIDTH = 31
N_BRANCH = 2
N_BUCKETS = 32
MAX_DISTANCE = 128
N_EXPERTS = 32
TOP_K_EXPERTS = 4
D_EXPERT = 1024
SWIGLU_LIMIT = 7.0
SWIGLU_ALPHA = 1.702
PLE_DIM = 256
LN_EPS = 1e-5
DEEPNORM_ALPHA = (2 * DEPTH) ** 0.25
DEEPNORM_BETA = (8 * DEPTH) ** -0.25

IN_SPLITS = [ATTN_WIDTH, ATTN_WIDTH, ATTN_WIDTH, IDX_HEADS * IDX_DIM, IDX_DIM, IDX_HEADS,
             2 * CONV_CH, D_MODEL, D_MODEL]
IN_COLS = sum(IN_SPLITS)

kernel_name = "hybrid_dsa_conformer_moe_block"

def layer_norm(x, g, b):
    xf = x.astype(jnp.float32)
    mu = jnp.mean(xf, axis=-1, keepdims=True)
    var = jnp.mean(jnp.square(xf - mu), axis=-1, keepdims=True)
    return ((xf - mu) * lax.rsqrt(var + LN_EPS) * g.astype(jnp.float32) + b.astype(jnp.float32)).astype(x.dtype)

def t5_bucket(rel):
    max_exact = N_BUCKETS // 2
    rel_f = jnp.maximum(rel, 1).astype(jnp.float32)
    large = max_exact + (jnp.log(rel_f / max_exact) / math.log(MAX_DISTANCE / max_exact)
                         * (N_BUCKETS - max_exact)).astype(jnp.int32)
    large = jnp.minimum(large, N_BUCKETS - 1)
    return jnp.where(rel < max_exact, rel, large)

def dsa_attention(q, k, v, q_idx, k_idx, w_idx, rel_bias):
    B, S = q.shape[0], q.shape[1]
    top_k = min(TOPK_MAX, S // 4)
    n_blocks = S // Q_BLOCK
    key_pos = jnp.arange(S, dtype=jnp.int32)
    gather_rows = jax.vmap(lambda arr, idx: arr[idx])

    def block(i):
        start = i * Q_BLOCK
        q_pos = start + jnp.arange(Q_BLOCK, dtype=jnp.int32)
        qb = lax.dynamic_slice_in_dim(q, start, Q_BLOCK, axis=1)
        qib = lax.dynamic_slice_in_dim(q_idx, start, Q_BLOCK, axis=1)
        wb = lax.dynamic_slice_in_dim(w_idx, start, Q_BLOCK, axis=1)
        dots = jnp.einsum('bqhd,bsd->bqhs', qib, k_idx, preferred_element_type=jnp.float32)
        score = jnp.einsum('bqh,bqhs->bqs', wb.astype(jnp.float32) * IDX_SCALE, jax.nn.relu(dots))
        causal = key_pos[None, :] <= q_pos[:, None]
        score = jnp.where(causal[None], score, -jnp.inf)
        _, sel = lax.top_k(score, top_k)
        valid = sel <= q_pos[None, :, None]
        k_sel = gather_rows(k, sel)
        v_sel = gather_rows(v, sel)
        rel = jnp.maximum(q_pos[None, :, None] - sel, 0)
        bias = jnp.transpose(rel_bias[t5_bucket(rel)], (0, 3, 1, 2))
        logits = jnp.einsum('bqhd,bqkhd->bhqk', qb, k_sel,
                            preferred_element_type=jnp.float32) * ATTN_SCALE + bias.astype(jnp.float32)
        logits = jnp.where(valid[:, None], logits, -jnp.inf)
        probs = jax.nn.softmax(logits, axis=-1)
        return jnp.einsum('bhqk,bqkhd->bqhd', probs.astype(v.dtype), v_sel)

    out = lax.map(block, jnp.arange(n_blocks, dtype=jnp.int32))
    return jnp.transpose(out, (1, 0, 2, 3, 4)).reshape(B, S, ATTN_WIDTH)

def conformer_conv(conv_in, w_dw, b_dw, ln_g, ln_b):
    a, g = jnp.split(conv_in, 2, axis=-1)
    u = a * jax.nn.sigmoid(g)
    y = lax.conv_general_dilated(u, w_dw[:, None, :], window_strides=(1,),
                                 padding=((CONV_WIDTH - 1, 0),),
                                 dimension_numbers=('NWC', 'WIO', 'NWC'),
                                 feature_group_count=CONV_CH) + b_dw
    y = layer_norm(y, ln_g, ln_b)
    return jax.nn.silu(y)

def mixing_sublayer(x, w_in, b_in, w_o_attn, w_dw, b_dw, conv_ln_g, conv_ln_b, w_o_conv, w_out, rel_bias):
    B, S, _ = x.shape
    proj = x @ w_in + b_in
    offsets = np.cumsum(IN_SPLITS)[:-1].tolist()
    q, k, v, qi, ki, wi, conv_in, g_attn, g_conv = jnp.split(proj, offsets, axis=-1)
    q = q.reshape(B, S, N_HEADS, HEAD_DIM)
    k = k.reshape(B, S, N_HEADS, HEAD_DIM)
    v = v.reshape(B, S, N_HEADS, HEAD_DIM)
    qi = qi.reshape(B, S, IDX_HEADS, IDX_DIM)
    y_attn = dsa_attention(q, k, v, qi, ki, wi, rel_bias) @ w_o_attn
    y_conv = conformer_conv(conv_in, w_dw, b_dw, conv_ln_g, conv_ln_b) @ w_o_conv
    merged = jax.nn.sigmoid(g_attn) * y_attn + jax.nn.sigmoid(g_conv) * y_conv
    return merged @ w_out

def moe_ffn(h, w_router, b_router, w_gate_up, b_gate_up, w_down, b_down):
    B, S, D = h.shape
    t = h.reshape(B * S, D)
    logits = (t @ w_router + b_router).astype(jnp.float32)
    top_vals, top_idx = lax.top_k(logits, TOP_K_EXPERTS)
    gates = jax.nn.softmax(top_vals, axis=-1)
    rows = jnp.arange(B * S)[:, None]
    combine = jnp.zeros((B * S, N_EXPERTS), jnp.float32).at[rows, top_idx].set(gates)
    out = jnp.zeros_like(t)
    for e in range(N_EXPERTS):
        gu = t @ w_gate_up[e] + b_gate_up[e]
        g, u = gu[:, :D_EXPERT], gu[:, D_EXPERT:]
        g = jnp.minimum(g, SWIGLU_LIMIT)
        u = jnp.clip(u, -SWIGLU_LIMIT, SWIGLU_LIMIT)
        act = (u + 1) * (g * jax.nn.sigmoid(SWIGLU_ALPHA * g))
        y = act @ w_down[e] + b_down[e]
        out = out + combine[:, e:e + 1].astype(t.dtype) * y
    return out.reshape(B, S, D)

def setup_inputs(seed: int = 0) -> dict:
    key = jax.random.key(seed)
    ks = jax.random.split(key, 26)
    f32 = jnp.float32

    def nrm(k, shape, fan_in, scale=1.0):
        return jax.random.normal(k, shape, f32) * (scale * fan_in ** -0.5)

    def small(k, shape, s=0.02):
        return jax.random.normal(k, shape, f32) * s

    L = DEPTH
    return {
        "x": jax.random.normal(ks[0], (BATCH, SEQ, D_MODEL), f32),
        "p": jax.random.normal(ks[1], (DEPTH, BATCH, SEQ, PLE_DIM), f32),
        "w_in": nrm(ks[2], (L, D_MODEL, IN_COLS), D_MODEL),
        "b_in": small(ks[3], (L, IN_COLS)),
        "w_o_attn": nrm(ks[4], (L, ATTN_WIDTH, D_MODEL), ATTN_WIDTH),
        "w_dw": nrm(ks[5], (L, CONV_WIDTH, CONV_CH), CONV_WIDTH),
        "b_dw": small(ks[6], (L, CONV_CH)),
        "conv_ln_g": 1.0 + small(ks[7], (L, CONV_CH)),
        "conv_ln_b": small(ks[8], (L, CONV_CH)),
        "w_o_conv": nrm(ks[9], (L, CONV_CH, D_MODEL), CONV_CH),
        "w_out": nrm(ks[10], (L, D_MODEL, D_MODEL), D_MODEL, DEEPNORM_BETA),
        "ln1_g": 1.0 + small(ks[11], (L, D_MODEL)),
        "ln1_b": small(ks[12], (L, D_MODEL)),
        "w_router": nrm(ks[13], (L, D_MODEL, N_EXPERTS), D_MODEL),
        "b_router": small(ks[14], (L, N_EXPERTS), 0.01),
        "w_gate_up": nrm(ks[15], (L, N_EXPERTS, D_MODEL, 2 * D_EXPERT), D_MODEL),
        "b_gate_up": small(ks[16], (L, N_EXPERTS, 2 * D_EXPERT)),
        "w_down": nrm(ks[17], (L, N_EXPERTS, D_EXPERT, D_MODEL), D_EXPERT, DEEPNORM_BETA),
        "b_down": small(ks[18], (L, N_EXPERTS, D_MODEL)),
        "w_ple_gate": nrm(ks[19], (L, D_MODEL, D_MODEL), D_MODEL),
        "w_ple_proj": nrm(ks[20], (L, PLE_DIM, D_MODEL), PLE_DIM, DEEPNORM_BETA),
        "ln2_g": 1.0 + small(ks[21], (L, D_MODEL)),
        "ln2_b": small(ks[22], (L, D_MODEL)),
        "rel_bias": small(ks[23], (N_BUCKETS, N_HEADS), 0.5),
    }

def reference(x, p, w_in, b_in, w_o_attn, w_dw, b_dw, conv_ln_g, conv_ln_b, w_o_conv, w_out,
              ln1_g, ln1_b, w_router, b_router, w_gate_up, b_gate_up, w_down, b_down,
              w_ple_gate, w_ple_proj, ln2_g, ln2_b, rel_bias):
    for i in range(DEPTH):
        mix = mixing_sublayer(x, w_in[i], b_in[i], w_o_attn[i], w_dw[i], b_dw[i], conv_ln_g[i],
                              conv_ln_b[i], w_o_conv[i], w_out[i], rel_bias)
        x = layer_norm(DEEPNORM_ALPHA * x + mix, ln1_g[i], ln1_b[i])
        h = DEEPNORM_ALPHA * x + moe_ffn(x, w_router[i], b_router[i], w_gate_up[i], b_gate_up[i],
                                         w_down[i], b_down[i])
        ple = jax.nn.sigmoid(h @ w_ple_gate[i]) * (p[i] @ w_ple_proj[i])
        x = layer_norm(h + ple, ln2_g[i], ln2_b[i])
    return x


_drawn_inputs = setup_inputs


def setup_inputs(seed=0):
    import zlib

    import numpy as np

    out = dict(_drawn_inputs(seed))
    spreads = {}
    factors = {'b_dw': 3.281,
     'conv_ln_g': 4.217,
     'conv_ln_b': 4.547,
     'b_router': 3.382,
     'b_gate_up': 8.0,
     'b_down': 6.627,
     'ln2_g': 2.748,
     'ln2_b': 2.828}
    for name, (base, spread) in spreads.items():
        noise = np.random.default_rng([zlib.crc32(name.encode()), seed]).standard_normal(out[name].shape)
        drawn = base * np.exp(spread * noise) if base else spread * noise
        out[name] = __import__('jax').numpy.asarray(drawn.astype(out[name].dtype))
    for name, factor in factors.items():
        out[name] = (out[name] * factor).astype(out[name].dtype)
    return out
```

```python
import concourse.bass as bass
from concourse import mybir
from contextlib import ExitStack
import math
import numpy as np

D, S, P = 1024, 256, 128
NT = S // P
KD = D // P
H, HD = 8, 64
TOPK = min(256, S // 4)
IDX_SCALE = (8 ** -0.5) * (64 ** -0.5)
CW, CC = 31, 512
NB = 32
NE, TOPE = 32, 4
PD = 256
CAP = 64
WIDE = 2 * CAP
LIMIT, SW_ALPHA = 7.0, 1.702
EPS = 1e-5
ALPHA = 2 ** 0.25
NEG = -1.0e30
BELOW = -3.0e38
TAKEN = -3.4e38

NMORE = (S - WIDE) // CAP
MORE = NMORE * NE
LIST = NT * P * TOPE // CAP

Q0, K0, V0, QI0 = 0, 512, 1024, 1536
KI0, WI0, CA0, CG0, GA0, GC0, IN_COLS = 2048, 2112, 2120, 2632, 3144, 4168, 5192

NS = 12
ES = 16
SLOT = 2048
CW256 = 256
FRONT = ([("in", QI0, 256), ("in", QI0 + 256, 256), ("in", KI0, 72)]
         + [("in", c, 256) for c in (Q0, Q0 + 256, K0, K0 + 256, V0, V0 + 256)]
         + [("in", c, 256) for c in (CA0, CG0, CA0 + 256, CG0 + 256)]
         + [("in", GA0 + 256 * j, 256) for j in range(4)] + [("in", GC0 + 256 * j, 256) for j in range(4)]
         + [("oa", 0, 512), ("oa", 512, 512), ("oc", 0, 512), ("oc", 512, 512)]
         + [("out", 256 * j, 256) for j in range(4)])
NF = len(FRONT)
CPE = 12
UNROLL = 4
assert UNROLL * CPE % ES == 0
TILES = ["qi"] * 4 + ["q"] * 4 + ["k"] * 4 + ["a", "a", "g", "g"] * 2 + ["ga"] * 8 + ["gc"] * 8


def rel_bucket_onehot():
    dist = (S - 1) - np.arange(S + P)
    d = np.maximum(dist, 1).astype(np.float32)
    large = 16 + (np.log(d / np.float32(16)) / np.float32(math.log(128 / 16)) * np.float32(16)).astype(np.int32)
    bucket = np.where(dist < 16, dist, np.minimum(large, NB - 1))
    return ((bucket[None, :] == np.arange(NB)[:, None]) & (dist >= 0)[None, :]).astype(np.float32)


BANK_ORDER = (0, 2, 1, 3)


def further_passes():
    return np.stack([np.repeat(WIDE + CAP * np.arange(NMORE), NE), np.tile(np.arange(NE), NMORE)], axis=1).astype(np.float32)


class Tally:

    def __init__(self, start=0):
        self.n = start

    def up(self, k=1):
        self.n += k
        return self.n


def program(nc, x, xT, pT, w_in, bT, bki, b_in, w_oa, w_oc, w_out, dwT, convT, ln1g, ln1b, w_r, b_r,
            w_gu, bguT, w_dn, b_dn, w_pg, w_pp, ln2g, ln2b, relb, onehot, passes, out, table):
    F32, I32, U32 = mybir.dt.float32, mybir.dt.int32, mybir.dt.uint32
    ALU, ACT, AX = mybir.AluOpType, mybir.ActivationFunctionType, mybir.AxisListType
    ctx = ExitStack()
    with ctx:
        def sb(name, shape, dt=F32):
            return ctx.enter_context(nc.sbuf_tensor(name, shape, dt))

        def sem(name):
            return ctx.enter_context(nc.semaphore(name))

        ring = sb("ring", [P, NS, SLOT])
        arena = sb("arena", [P, 27400])
        bank = [ctx.enter_context(nc.psum_tensor(f"bank{i}", [P, 512], F32)) for i in range(8)]

        def view(at, n):
            return arena[:, at:at + n]

        x1 = view(0, 2048).rearrange("p (t d) -> p t d", t=NT)
        acc = view(2048, 2048).rearrange("p (t d) -> p t d", t=NT)
        pple = view(4096, 2048).rearrange("p (t d) -> p t d", t=NT)
        xT_sb = view(4096, 2048).rearrange("p (k t) -> p k t", k=KD)
        x_sb = x1
        qT = view(6144, 1024).rearrange("p (a t) -> p a t", a=4)
        kT = view(7168, 1024).rearrange("p (a t) -> p a t", a=4)
        qiT = view(8192, 1024).rearrange("p (a t) -> p a t", a=4)
        kiT = view(9216, 256)
        v_sb = view(9472, 1024).rearrange("p (t c) -> p t c", t=NT)
        U = CW - 1 + S
        u_sb = view(10496, 4 * U).rearrange("p (a t) -> p a t", a=4)
        cy = view(11640, 1024).rearrange("p (a t) -> p a t", a=4)
        cg = view(12664, 1024).rearrange("p (a t) -> p a t", a=4)
        sga = view(13688, 2048).rearrange("p (a t) -> p a t", a=KD)
        sgc = view(15736, 2048).rearrange("p (a t) -> p a t", a=KD)
        logit = view(17784, 3072).rearrange("p (h s) -> p h s", h=H)
        hankel = view(20856, 2048).rearrange("p (h s) -> p h s", h=H)
        score = view(22904, 384)
        rest = view(23288, 384)
        amask = view(23672, 384)
        relu = view(24056, 768).rearrange("p (b s) -> p b s", b=2)
        pT_h = view(24056, 768).rearrange("p (b s) -> p b s", b=2)
        attnT = view(8192, 1024).rearrange("p (a t) -> p a t", a=4)
        merged = acc.rearrange("p t d -> p (t d)").rearrange("p (a t) -> p a t", a=KD)
        lng1 = view(19832, 1024)
        lnb1 = view(12664, 1024)
        extra = [view(at, SLOT) for at in (13688, 15736, 17784, 20856)]
        res = view(6144, 2048).rearrange("p (t d) -> p t d", t=NT)
        x1T = view(8192, 2048).rearrange("p (k t) -> p k t", k=KD)
        mean = view(9216, 256)
        std = view(22904, 256)
        o = 6144
        XT = view(o, 1024).rearrange("p (k q c) -> p k q c", k=KD, q=2)
        hsb = view(o + 1024, 2048)
        gt = view(o + 3072, 512).rearrange("p (f c) -> p f c", f=8)
        up = view(o + 3584, 512).rearrange("p (f c) -> p f c", f=8)
        sg = view(o + 4096, 512).rearrange("p (f c) -> p f c", f=8)
        act_sb = view(o + 4608, 512).rearrange("p (f c) -> p f c", f=8)
        ysb = view(o + 5120, 1024)
        G2 = view(o + 6144, 512).rearrange("p (q t) -> p q t", q=2)
        sel = view(o + 6656, 256).rearrange("p (t q c) -> p t q c", t=NT, q=2)
        XT_w = view(19832, 1024).rearrange("p (k c) -> p k c", k=KD)
        act_w = view(22904, 1024).rearrange("p (f c) -> p f c", f=8)
        gt_w, up_w, sg_w = (view(o + at, 512).rearrange("p (f c) -> p f c", f=4) for at in (3072, 3584, 4096))
        sel_w = view(o + 6656, 256).rearrange("p (t c) -> p t c", t=NT)
        hT = view(13688, 2048).rearrange("p (k t) -> p k t", k=KD)
        pge = view(15736, 2048).rearrange("p (t d) -> p t d", t=NT)
        lng2, lnb2 = view(7168, 1024), view(8192, 1024)
        o = 24824
        ident, flip, upper, ones = (view(o + P * j, P) for j in range(4))
        o += 512
        iota_e = view(o + 64, NE)
        bT_sb = view(o + 96, 36)
        bq = view(o + 132, 4)
        bki_sb = view(o + 136, 1)
        dw = view(o + 137, 124).rearrange("p (a j) -> p a j", a=4)
        cv = view(o + 261, 12).rearrange("p (j a) -> p j a", j=3)
        wsc = view(o + 273, 16).rearrange("p (t h) -> p t h", t=NT)
        bwi = view(o + 289, 8)
        top8 = view(o + 297, 16).rearrange("p (t h) -> p t h", t=NT)
        idx8 = view(o + 313, 16).rearrange("p (t h) -> p t h", t=NT)
        stats = view(o + 329, 24).rearrange("p (t a b) -> p t a b", t=NT, a=2)
        mv = view(o + 353, 4).rearrange("p (t h) -> p t h", t=NT)
        rstd = view(o + 357, 2)
        mx = view(o + 359, 16).rearrange("p (t h) -> p t h", t=NT)
        ssum = view(o + 375, 16).rearrange("p (t h) -> p t h", t=NT)
        epsc = view(o + 391, 1)
        NEP = NE + 2
        mask = view(o + 392, NT * NEP).rearrange("p (t e) -> p t e", t=NT)
        gate = view(o + 460, NT * NEP).rearrange("p (t e) -> p t e", t=NT)
        slot1 = view(o + 528, NT * NEP).rearrange("p (t e) -> p t e", t=NT)
        rl = view(o + 596, NT * NE).rearrange("p (t e) -> p t e", t=NT)
        br = view(o + 660, NE)
        bgu = view(o + 692, NE * 16).rearrange("p (e f) -> p e f", e=NE)
        selg = view(o + 1204, 512).rearrange("p (q t h c) -> p q t h c", q=2, t=NT, h=2)
        need = view(o + 1716, 1)[0:MORE, :]
        pass_c = view(o + 1717, 2)[0:MORE, :]
        above, expert_no = pass_c[:, 0:1], pass_c[:, 1:2]
        place = view(o + 1719, LIST)[0:MORE, :]
        iota_c = view(o + 1735, WIDE)
        wide_f = view(o + 1863, NE)[0:1, :]
        assert o + 1895 <= 27400
        relb_sb = sb("relb_sb", [NB, H])
        oneh_sb = sb("oneh_sb", [NB, S + P])
        tab_sb = sb("tab_sb", [H, S + P])
        wr_sb = sb("wr_sb", [P, KD, NE])
        idxu = sb("idxu", [P, NT, 8], U32)
        more = sb("more", [1, LIST + 1], I32)
        wide = sb("wide", [1, NE], I32)
        pT_sb = view(10496, 512).rearrange("p (k t) -> p k t", k=2)
        wpp_sb = view(6144, 2048).rearrange("p (k d) -> p k d", k=2)
        vb = view(13688, 512)

        e_in = [sem(f"expert_slot{i}_in") for i in range(ES)]
        arrived = [sem(f"slot{i}_arrived") for i in range(NS)]
        chunk_used = sem("chunk_used")
        small_in, late_in = sem("small_in"), sem("late_in")
        xT_in, x_in = sem("xT_in"), sem("x_in")
        relb_in = sem("relb_in")
        tab_out, hankel_in, ln_in = sem("tab_out"), sem("hankel_in"), sem("ln_in")
        consts = sem("consts")
        pool_chain = sem("pool_chain")
        v_chain = sem("v_chain")
        a_chain = sem("a_chain")
        tile_done, tile_out = sem("tile_done"), sem("tile_out")
        wi_done, wi_out = sem("wi_done"), sem("wi_out")
        dots_done, relu_out, relu_used = sem("dots_done"), sem("relu_out"), sem("relu_used")
        score_masked = sem("score_masked")
        chosen, amask_ready = sem("chosen"), sem("amask_ready")
        v_done, v_out = sem("v_done"), sem("v_out")
        tab_done, tab_ready = sem("tab_done"), sem("tab_ready")
        lg_done, lg_out = sem("lg_done"), sem("lg_out")
        max_ready, exp_ready, probs_ready = sem("max_ready"), sem("exp_ready"), sem("probs_ready")
        pt_done, pt_out, pv_done, attn_out = sem("pt_done"), sem("pt_out"), sem("pv_done"), sem("attn_out")
        bq_ready = sem("bq_ready")
        ple_in, pple_done, pple_out = sem("ple_in"), sem("pple_done"), sem("pple_out")
        conv_y, mean_done, sq_ready, var_done = sem("conv_y"), sem("mean_done"), sem("sq_ready"), sem("var_done")
        centred = sem("centred")
        vareps_ready, std_ready, norm_ready, csig_ready, conv_ready = (
            sem("vareps_ready"), sem("std_ready"), sem("norm_ready"), sem("csig_ready"), sem("conv_ready"))
        y_done, y_out, merged_ready = sem("y_done"), sem("y_out"), sem("merged_ready")
        mix_done = sem("mix_done")
        var1, std1, x1_ready = sem("var1"), sem("std1"), sem("x1_ready")
        xt_done, x1T_out = sem("x1T_done"), sem("x1T_out")
        rl_done, rl_shift, rl_exp = sem("rl_done"), sem("rl_shift"), sem("rl_exp")
        mask_ready, cum_done, more_ready = sem("mask_ready"), sem("cum_done"), sem("more_ready")
        rank_done, list_done = sem("rank_done"), sem("list_done")

        slot_moved = sem("slot_moved")
        wide_ready = sem("wide_ready")
        selw_ready, gathw_done, xtw_ready = sem("selw_ready"), sem("gathw_done"), sem("xtw_ready")
        selw_onehot = sem("selw_onehot")
        selg_ready, selg_part, sel_ready = sem("selg_ready"), sem("selg_part"), sem("sel_ready")
        gath_done, xt_half, xt_ready = sem("gath_done"), sem("xt_half"), sem("xt_ready")
        gT_done, acc_out = sem("gT_done"), sem("acc_out")
        first_zero, first_rows = sem("first_zero"), sem("first_rows")
        sgt_done, g2_out, gu_done, h_out = sem("sgt_done"), sem("g2_out"), sem("gu_done"), sem("h_out")
        comb_done, t_done, t_read = sem("comb_done"), sem("t_done"), sem("t_read")
        sw_biased, sw_summed, sw_prod = sem("sw_biased"), sem("sw_summed"), sem("sw_prod")
        sig_in, sig_out, act_ready = sem("sig_in"), sem("sig_out"), sem("act_ready")
        d_done, y_half, y_sb_out = sem("d_done"), sem("y_half"), sem("y_sb_out")
        hT_done, hT_out, pg_done, pge_ready = sem("hT_done"), sem("hT_out"), sem("pg_done"), sem("pge_ready")
        var2, std2, t_chain, out_ready, out_done = (
            sem("var2"), sem("std2"), sem("t_chain"), sem("out_ready"), sem("out_done"))

        def wslot(i):
            return ring[:, i % NS, :]

        def w_view(i):
            what, _, n = FRONT[i]
            kt = 4 if what in ("oa", "oc") else KD
            return wslot(i)[:, 0:kt * n].rearrange("p (k c) -> p k c", k=kt)

        src = {"in": w_in, "oa": w_oa, "oc": w_oc, "out": w_out}

        def wait_chunk(eng, i):
            eng.wait_ge(arrived[i % NS], 16 * (i // NS + 1))

        def front_used(i):
            what, c0, n = FRONT[i]
            if c0 == KI0:
                return wi_done, 2
            if c0 in (V0, V0 + 256) and what == "in":
                return v_done, 2 + 2 * (c0 > V0)
            if what == "in":
                return tile_done, 2 * sum(w == "in" and b != KI0 and not V0 <= b < QI0 for w, b, _ in FRONT[:i + 1])
            if what == "out":
                return mix_done, 2 + c0 // 256
            return y_done, 4 * (i - FRONT.index(("oa", 0, 512)) + 1)

        def expert_used(e, c):
            if c == KD - 1:
                return gu_done, e * 4 + 4
            if c == CPE - 1:
                return d_done, e + 1
            return chunk_used, e * (CPE - 2) + (c + 1 if c < KD else c)

        def expert_w(q, c):
            i = (q * CPE + c) % ES
            return ring[:, (NF + i) % NS, :] if i < NS else extra[i - NS]

        def expert_source(e, c):
            if c < KD:
                return w_gu[bass.ds(e, 1), c * P:(c + 1) * P, :].rearrange("e p d -> p (e d)")
            f = 2 * (c - KD)
            return w_dn[bass.ds(e, 1), f * P:(f + 2) * P, :].rearrange("e (k p) d -> p (e k) d", p=P)

        def load_expert(sp, e, q, c):
            w = expert_w(q, c)
            if c >= KD:
                w = w.rearrange("p (k d) -> p k d", k=2)
            sp.dma_start(w, expert_source(e, c)).then_inc(e_in[(q * CPE + c) % ES], 16)

        def expert_in(step, q, c):
            n = q * CPE + c
            return e_in[n % ES], step * (16 * UNROLL * CPE // ES) + 16 * (n // ES + 1)

        with nc.Block() as block:
            @block.sync
            def _(sp):
                sp.dma_start(xT_sb, xT.rearrange("(k p) t -> p k t", p=P)).then_inc(xT_in, 16)
                for i, (what, c0, n) in enumerate(FRONT):
                    if i >= NS:
                        sp.wait_ge(*front_used(i - NS))
                    sp.dma_start(w_view(i), src[what][:, c0:c0 + n].rearrange("(k p) c -> p k c", p=P)
                                 ).then_inc(arrived[i % NS], 16)
                for c in range(CPE):
                    sp.wait_ge(*front_used(NF + c - NS))
                    load_expert(sp, 0, 0, c)
                for c, free in enumerate(((y_out, 8), (merged_ready, 8), (pt_done, 8), (lg_done, 8))):
                    sp.wait_ge(*free)
                    load_expert(sp, 1, 1, c)

            @block.gpsimd
            def _(g):
                n = Tally()
                g.memset(ident, 0.0).then_inc(pool_chain, 1)
                g.memset(flip, 0.0).then_inc(pool_chain, 1)
                g.memset(upper, 1.0).then_inc(pool_chain, 1)
                g.memset(u_sb[:, :, 0:CW - 1], 0.0).then_inc(consts, 1)
                g.memset(ones, 1.0).then_inc(consts, 1)
                g.memset(epsc, EPS).then_inc(consts, 1)
                g.memset(mask[:, :, :], 0.0).then_inc(consts, 1)
                g.memset(gate[:, :, :], 0.0).then_inc(consts, 1)
                g.memset(slot1[:, :, :], 0.0).then_inc(consts, 1)
                g.iota(iota_c, [[1, WIDE]], base=1, channel_multiplier=0,
                       allow_small_or_imprecise_dtypes=True).then_inc(consts, 1)
                g.iota(iota_e, [[1, NE]], base=0, channel_multiplier=0,
                       allow_small_or_imprecise_dtypes=True).then_inc(consts, 1)
                g.wait_ge(pool_chain, 3)
                g.affine_select(out=ident, in_=ident, compare_op=ALU.not_equal, fill=1.0, base=0,
                                pattern=[[-1, P]], channel_multiplier=1).then_inc(consts, 1)
                g.affine_select(out=flip, in_=flip, compare_op=ALU.not_equal, fill=1.0, base=-(P - 1),
                                pattern=[[1, P]], channel_multiplier=1).then_inc(consts, 1)
                g.affine_select(out=upper, in_=upper, compare_op=ALU.is_gt, fill=0.0, base=0,
                                pattern=[[1, P]], channel_multiplier=-1).then_inc(consts, 1)
                g.wait_ge(tab_ready, 1)
                g.dma_start(table, tab_sb[:, :]).then_inc(tab_out, 16)
                g.wait_ge(tab_out, 16)
                skew = bass.AP(tensor=table.tensor, offset=0, ap=[[1, P], [S + P, H], [1, S]])
                g.dma_start(hankel, skew).then_inc(hankel_in, 16)
                g.wait_ge(relu_used, 2 * H)
                g.affine_select(out=score[:, 0:P], in_=score[:, 0:P], compare_op=ALU.is_ge, fill=BELOW,
                                base=0, pattern=[[-1, P]], channel_multiplier=1).then_inc(score_masked, 1)
                g.affine_select(out=score[:, P:3 * P], in_=score[:, P:3 * P], compare_op=ALU.is_ge, fill=BELOW,
                                base=P, pattern=[[-1, S]], channel_multiplier=1).then_inc(score_masked, 1)
                g.wait_ge(chosen, 1)
                g.affine_select(out=amask[:, 0:P], in_=amask[:, 0:P], compare_op=ALU.is_ge, fill=NEG,
                                base=0, pattern=[[-1, P]], channel_multiplier=1).then_inc(amask_ready, 1)
                g.affine_select(out=amask[:, P:3 * P], in_=amask[:, P:3 * P], compare_op=ALU.is_ge, fill=NEG,
                                base=P, pattern=[[-1, S]], channel_multiplier=1).then_inc(amask_ready, 1)

            @block.tensor
            def _(pe):
                tiles = Tally()

                pe.wait_ge(xT_in, 16)
                pe.wait_ge(relb_in, 32)
                pe.matmul(bank[7][0:H, 0:S + P], relb_sb[:, :], oneh_sb[:, :], start=True, stop=True).then_inc(tab_done, 1)

                def two(i):
                    wait_chunk(pe, i)
                    for j in range(2):
                        n = tiles.n
                        if n >= 4:
                            pe.wait_ge(tile_out, n - 3)
                        w = w_view(i)
                        for k in range(KD):
                            mm = pe.matmul(bank[n % 4][:, 0:S], w[:, k, j * P:(j + 1) * P], xT_sb[:, k, :],
                                           start=(k == 0), stop=(k == KD - 1))
                        mm.then_inc(tile_done, 1)
                        tiles.up()

                two(0)
                two(1)
                wait_chunk(pe, 2)
                w = w_view(2)
                for half in range(2):
                    for k in range(KD):
                        mm = pe.matmul(bank[6][half * 64:half * 64 + 64, 0:S], w[:, k, 0:64], xT_sb[:, k, :],
                                       start=(k == 0), stop=(k == KD - 1))
                mm.then_inc(wi_done, 1)
                pe.wait_ge(tab_ready, 1)
                for t in range(NT):
                    for k in range(KD):
                        mm = pe.matmul(bank[7][:, t * 8:t * 8 + 8], xT_sb[:, k, t * P:(t + 1) * P], w[:, k, 64:72],
                                       start=(k == 0), stop=(k == KD - 1))
                mm.then_inc(wi_done, 1)
                two(3)
                pe.wait_ge(tile_out, 4)
                pe.wait_ge(wi_out, 2)
                for h in range(H):
                    if h >= 4:
                        pe.wait_ge(relu_out, h - 3)
                    a = (h % 2) * 64
                    b = bank[4 + h % 4]
                    pe.matmul(b[:, 0:P], qiT[a:a + 64, h // 2, 0:P], kiT[a:a + 64, 0:P], start=True, stop=True)
                    pe.matmul(b[:, P:3 * P], qiT[a:a + 64, h // 2, P:S], kiT[a:a + 64, 0:S],
                              start=True, stop=True).then_inc(dots_done, 1)
                two(4)
                two(5)
                two(6)
                pe.wait_ge(relu_out, 8)
                for j in range(2):
                    wait_chunk(pe, 7 + j)
                    for t in range(NT):
                        for k in range(KD):
                            mm = pe.matmul(bank[4 + 2 * j + t][:, 0:256], xT_sb[:, k, t * P:(t + 1) * P],
                                           w_view(7 + j)[:, k, :], start=(k == 0), stop=(k == KD - 1))
                        mm.then_inc(v_done, 1)
                two(9)
                pe.wait_ge(tile_out, 12)
                pe.wait_ge(hankel_in, 16)
                for h in range(H):
                    if h < 4:
                        pe.wait_ge(v_out, h + 1)
                    else:
                        pe.wait_ge(lg_out, h - 3)
                    a = (h % 2) * 64
                    b = bank[4 + h % 4]
                    pe.matmul(b[:, 0:P], qT[a:a + 64, h // 2, 0:P], kT[a:a + 64, h // 2, 0:P], start=True, stop=False)
                    pe.matmul(b[:, 0:P], flip, hankel[:, h, P:S], start=False, stop=True)
                    pe.matmul(b[:, P:3 * P], qT[a:a + 64, h // 2, P:S], kT[a:a + 64, h // 2, :], start=True, stop=False)
                    pe.matmul(b[:, P:3 * P], flip, hankel[:, h, :], start=False, stop=True).then_inc(lg_done, 1)
                for i in range(10, 21):
                    two(i)
                pe.wait_ge(conv_y, 1)
                for a in range(4):
                    mm = pe.matmul(bank[7][:, 0:S], ones, cy[:, a, :], start=(a == 0), stop=(a == 3))
                mm.then_inc(mean_done, 1)
                pe.wait_ge(probs_ready, 2)
                pe.wait_ge(lg_out, 8)
                for h in range(H + 1):
                    if h < H:
                        if h >= 2:
                            pe.wait_ge(pt_out, h - 1)
                        for j, at in enumerate((0, P, 2 * P)):
                            mm = pe.transpose(bank[4 + h % 2][:, j * P:(j + 1) * P], logit[:, h, at:at + P], ident)
                        mm.then_inc(pt_done, 1)
                    if h >= 1:
                        g = h - 1
                        pe.wait_ge(pt_out, g + 1)
                        if g >= 4 and g % 2 == 0:
                            pe.wait_ge(attn_out, g // 2 - 1)
                        if g == 2:
                            pe.wait_ge(centred, 1)
                        a = (g % 2) * 64
                        b = bank[6 + (g // 2) % 2]
                        vg = slice(g * 64, g * 64 + 64)
                        pe.matmul(b[a:a + 64, 0:P], v_sb[:, 0, vg], pT_h[:, g % 2, 0:P], start=True, stop=True)
                        pe.matmul(b[a:a + 64, P:S], v_sb[:, 0, vg], pT_h[:, g % 2, P:S], start=True, stop=False)
                        pe.matmul(b[a:a + 64, P:S], v_sb[:, 1, vg], pT_h[:, g % 2, S:S + P],
                                  start=False, stop=True).then_inc(pv_done, 1)
                pe.wait_ge(sq_ready, 1)
                for a in range(4):
                    mm = pe.matmul(bank[5][:, 0:S], ones, cg[:, a, :], start=(a == 0), stop=(a == 3))
                mm.then_inc(var_done, 1)
                pe.wait_ge(attn_out, 4)
                pe.wait_ge(tile_out, 36)

                def project(i0, rhs, n0):
                    for c in range(8):
                        i = i0 + c // 4
                        if c % 4 == 0:
                            wait_chunk(pe, i)
                        n = n0 + c
                        if n >= 4:
                            pe.wait_ge(y_out, n - 3)
                        for k in range(4):
                            mm = pe.matmul(bank[n % 4][:, 0:S], w_view(i)[:, k, (c % 4) * P:(c % 4 + 1) * P],
                                           rhs[:, k, :], start=(k == 0), stop=(k == 3))
                        mm.then_inc(y_done, 1)
                project(21, attnT, 0)
                pe.wait_ge(ple_in, 32)
                for n in range(4):
                    t, j = n // 2, n % 2
                    if n >= 2:
                        pe.wait_ge(pple_out, n - 1)
                    for k in range(2):
                        mm = pe.matmul(bank[6 + j][:, :], pT_sb[:, k, t * P:(t + 1) * P],
                                       wpp_sb[:, k, j * 512:(j + 1) * 512], start=(k == 0), stop=(k == 1))
                    mm.then_inc(pple_done, 1)
                pe.wait_ge(conv_ready, 1)
                project(23, cy, 8)
                pe.wait_ge(pple_out, 4)
                pe.wait_ge(merged_ready, 8)
                for t in range(NT):
                    for j in range(4):
                        if t == 0:
                            wait_chunk(pe, 25 + j)
                        for k in range(KD):
                            mm = pe.matmul(bank[4 + 2 * t + j // 2][:, (j % 2) * 256:(j % 2) * 256 + 256],
                                           merged[:, k, t * P:(t + 1) * P], w_view(25 + j)[:, k, :],
                                           start=(k == 0), stop=(k == KD - 1))
                        if t == 1 or j == 3:
                            mm.then_inc(mix_done, 1)
                for t in range(NT):
                    pe.wait_ge(x1_ready, t + 1)
                    for k in range(KD):
                        mm = pe.transpose(bank[2 * t + k // 4][:, (k % 4) * P:(k % 4 + 1) * P],
                                          x1[:, t, k * P:(k + 1) * P], ident)
                    mm.then_inc(xt_done, 1)
                for t in range(NT):
                    pe.wait_ge(x1T_out, t + 1)
                    for k in range(KD):
                        mm = pe.matmul(bank[4 + t][:, 0:NE], x1T[:, k, t * P:(t + 1) * P],
                                       wr_sb[:, k, :], start=(k == 0), stop=(k == KD - 1))
                    mm.then_inc(rl_done, 1)
                pe.wait_ge(mask_ready, 2)
                pe.matmul(bank[6][:, 0:NE], upper, mask[:, 0, 0:NE], start=True, stop=True)
                pe.matmul(bank[6][:, NE:2 * NE], upper, mask[:, 1, 0:NE], start=True, stop=False)
                pe.matmul(bank[6][:, NE:2 * NE], ones, mask[:, 0, 0:NE], start=False, stop=True)
                for t in range(NT):
                    pe.matmul(bank[6][0:1, 2 * NE:3 * NE], ones[:, 0:1], mask[:, t, 0:NE], start=(t == 0), stop=(t == NT - 1))
                for j in range(NMORE):
                    for t in range(NT):
                        mm = pe.matmul(bank[7][j * NE:(j + 1) * NE, 0:1], mask[:, t, 0:NE], ones[:, 0:1],
                                       start=(t == 0), stop=(t == NT - 1))
                mm.then_inc(cum_done, 1)
                pe.wait_ge(more_ready, 1)
                pe.matmul(bank[4][0:MORE, 0:1], upper[0:MORE, 0:MORE], need, start=True, stop=True).then_inc(rank_done, 1)
                pe.wait_ge(more_ready, 2)
                pe.matmul(bank[5][0:1, 0:LIST], expert_no, place, start=True, stop=True)
                pe.matmul(bank[5][0:1, LIST:LIST + 1], need, ones[0:MORE, 0:1], start=True, stop=True
                          ).then_inc(list_done, 1)

            @block.scalar
            def _(a):
                a.dma_start(relb_sb[:, :], relb).then_inc(relb_in, 16)
                a.dma_start(oneh_sb[:, :], onehot).then_inc(relb_in, 16)
                a.dma_start(bT_sb, bT).then_inc(small_in, 16)
                a.dma_start(bki_sb, bki).then_inc(small_in, 16)
                a.dma_start(bwi, b_in[WI0:WI0 + 8].partition_broadcast(P)).then_inc(small_in, 16)
                a.dma_start(pass_c, passes).then_inc(small_in, 16)
                a.dma_start(vb, b_in[V0:V0 + 512].partition_broadcast(P)).then_inc(late_in, 16)
                a.dma_start(dw, dwT.rearrange("p (a j) -> p a j", a=4)).then_inc(late_in, 16)
                a.dma_start(cv, convT.rearrange("p (j a) -> p j a", j=3)).then_inc(late_in, 16)
                a.dma_start(wr_sb[:, :, :], w_r.rearrange("(k p) e -> p k e", p=P)).then_inc(late_in, 16)
                a.dma_start(br, b_r.partition_broadcast(P)).then_inc(late_in, 16)
                a.dma_start(bgu, bguT.rearrange("p (e f) -> p e f", e=NE)).then_inc(late_in, 16)
                a.dma_start(x_sb, x.rearrange("(t p) d -> p t d", p=P)).then_inc(x_in, 16)
                a.wait_ge(tab_done, 1)
                a.activation(tab_sb[:, :], bank[7][0:H, 0:S + P], ACT.Identity).then_inc(tab_ready, 1)
                a.wait_ge(small_in, 16 * 4)

                cnt = Tally()

                def evac(dst, func, bias, scale=1.0):
                    n = cnt.n
                    a.wait_ge(tile_done, n + 1)
                    a.activation(dst, bank[n % 4][:, 0:S], func, bias=bias, scale=scale).then_inc(tile_out, 1)
                    cnt.up()

                for j in range(4):
                    evac(qiT[:, j, :], ACT.Identity, bT_sb[:, j:j + 1])
                a.wait_ge(wi_done, 1)
                a.activation(kiT, bank[6][:, 0:S], ACT.Identity, bias=bki_sb).then_inc(wi_out, 1)
                a.wait_ge(bq_ready, 1)
                for j in range(2):
                    evac(qT[:, j, :], ACT.Identity, bq[:, j:j + 1], 0.125)
                for h in range(H):
                    a.wait_ge(dots_done, h + 1)
                    if h >= 2:
                        a.wait_ge(relu_used, 2 * h - 2)
                    a.activation(relu[:, h % 2, :], bank[4 + h % 4][:, 0:3 * P], ACT.Relu).then_inc(relu_out, 1)
                for j in range(2, 4):
                    evac(qT[:, j, :], ACT.Identity, bq[:, j:j + 1], 0.125)
                for j in range(4):
                    evac(kT[:, j, :], ACT.Identity, bT_sb[:, 8 + j:9 + j])

                def conv_pair(c):
                    for j in range(2):
                        evac(cy[:, 2 * c + j, :], ACT.Identity, bT_sb[:, 12 + 2 * c + j:13 + 2 * c + j])
                    for j in range(2):
                        evac(cg[:, 2 * c + j, :], ACT.Sigmoid, bT_sb[:, 16 + 2 * c + j:17 + 2 * c + j])

                conv_pair(0)
                conv_pair(1)
                for j in range(2):
                    evac(sga[:, j, :], ACT.Sigmoid, bT_sb[:, 20 + j:21 + j])
                a.wait_ge(max_ready, 2)
                for h in range(H):
                    for t, (lo, n) in enumerate(((0, P), (P, S))):
                        a.activation(logit[:, h, lo:lo + n], logit[:, h, lo:lo + n], ACT.Exp,
                                     bias=mx[:, t, h:h + 1], accum_out=ssum[:, t, h:h + 1]).then_inc(exp_ready, 1)
                for j in range(2, 8):
                    evac(sga[:, j, :], ACT.Sigmoid, bT_sb[:, 20 + j:21 + j])
                for j in range(8):
                    evac(sgc[:, j, :], ACT.Sigmoid, bT_sb[:, 28 + j:29 + j])
                a.dma_start(wpp_sb, w_pp.rearrange("(k p) d -> p k d", p=P)).then_inc(ple_in, 16)
                a.wait_ge(conv_y, 1)
                a.dma_start(pT_sb, pT.rearrange("(k p) t -> p k t", p=P)).then_inc(ple_in, 16)
                for h in range(H):
                    if h == 2:
                        a.wait_ge(centred, 1)
                        a.activation(cg, cy, ACT.Square).then_inc(sq_ready, 1)
                    a.wait_ge(pt_done, h + 1)
                    if h >= 2:
                        a.wait_ge(pv_done, h - 1)
                    a.activation(pT_h[:, h % 2, :], bank[4 + h % 2][:, 0:3 * P], ACT.Identity).then_inc(pt_out, 1)
                    if h % 2 == 1:
                        a.wait_ge(pv_done, h + 1)
                        a.activation(attnT[:, h // 2, :], bank[6 + (h // 2) % 2][:, 0:S], ACT.Identity
                                     ).then_inc(attn_out, 1)
                a.wait_ge(var_done, 1)
                a.activation(std, bank[5][:, 0:S], ACT.Sqrt, bias=epsc, scale=1.0 / CC).then_inc(std_ready, 1)
                a.dma_start(lng1, ln1g.partition_broadcast(P)).then_inc(ln_in, 16)
                a.wait_ge(norm_ready, 4)
                a.activation(cg, cy, ACT.Sigmoid).then_inc(csig_ready, 1)
                for j in range(4):
                    a.wait_ge(pple_done, j + 1)
                    a.activation(pple[:, j // 2, (j % 2) * 512:(j % 2) * 512 + 512], bank[6 + j % 2][:, :], ACT.Identity
                                 ).then_inc(pple_out, 1)
                a.wait_ge(conv_ready, 1)
                a.dma_start(lnb1, ln1b.partition_broadcast(P)).then_inc(ln_in, 16)
                for t in range(NT):
                    a.wait_ge(var1, t + 1)
                    a.activation(rstd[:, t:t + 1], mv[:, t, 1:2], ACT.Sqrt, bias=epsc).then_inc(std1, 1)
                for t in range(NT):
                    a.wait_ge(xt_done, t + 1)
                    for b in range(2):
                        i = a.activation(x1T[:, 4 * b:4 * b + 4, t * P:(t + 1) * P],
                                         bank[2 * t + b][:, :].rearrange("p (k t) -> p k t", k=4), ACT.Identity)
                        if b == 1:
                            i.then_inc(x1T_out, 1)
                        else:
                            i.then_inc(a_chain, 1)
                a.wait_ge(rl_shift, 2)
                a.activation(rl[:, :, :], rl[:, :, :], ACT.Exp).then_inc(rl_exp, 1)

            @block.vector
            def _(v):
                c = Tally()
                v.wait_ge(small_in, 16 * 4)
                nc.vector.tensor_scalar(bq, bT_sb[:, 4:8], 0.125, None, ALU.mult).then_inc(bq_ready, 1)
                v.wait_ge(wi_done, 2)
                nc.vector.tensor_tensor(wsc, bank[7][:, 0:16].rearrange("p (t h) -> p t h", t=NT),
                                        bwi.unsqueeze(1).to_broadcast([P, NT, 8]), ALU.add).then_inc(v_chain, 1)
                v.wait_ge(v_chain, c.up())
                nc.vector.tensor_scalar(wsc, wsc, IDX_SCALE, None, ALU.mult).then_inc(wi_out, 1)
                v.wait_ge(wi_out, 2)
                for h in range(H):
                    v.wait_ge(relu_out, h + 1)
                    for t, (lo, n) in enumerate(((0, P), (P, S))):
                        if h == 0:
                            i = nc.vector.tensor_scalar(score[:, lo:lo + n], relu[:, 0, lo:lo + n],
                                                        wsc[:, t, 0:1], None, ALU.mult)
                        else:
                            v.wait_ge(relu_used, 2 * h - 1 + t)
                            i = nc.vector.scalar_tensor_tensor(score[:, lo:lo + n], relu[:, h % 2, lo:lo + n],
                                                               wsc[:, t, h:h + 1], score[:, lo:lo + n],
                                                               ALU.mult, ALU.add)
                        i.then_inc(relu_used, 1)
                v.wait_ge(score_masked, 2)
                for r in range(TOPK // 8):
                    for t, (lo, n) in enumerate(((0, P), (P, S))):
                        if r:
                            v.wait_ge(v_chain, c.n - 1)
                        now = rest if r else score
                        nc.vector.max(top8[:, t, :], now[:, lo:lo + n]).then_inc(v_chain, 1)
                        v.wait_ge(v_chain, c.up())
                        nc.vector.match_replace(rest[:, lo:lo + n], top8[:, t, :], now[:, lo:lo + n],
                                                TAKEN).then_inc(v_chain, 1)
                        c.up()
                v.wait_ge(v_chain, c.n)
                nc.vector.tensor_scalar(amask, rest, -3.2e38, NEG, ALU.is_gt, ALU.mult).then_inc(chosen, 1)
                v.wait_ge(late_in, 16 * 6)
                for n in range(4):
                    j, t = n // 2, n % 2
                    v.wait_ge(v_done, n + 1)
                    nc.vector.tensor_tensor(v_sb[:, t, j * 256:(j + 1) * 256], bank[4 + 2 * j + t][:, 0:256],
                                            vb[:, j * 256:(j + 1) * 256], ALU.add).then_inc(v_out, 1)
                v.wait_ge(amask_ready, 2)
                for h in range(H):
                    v.wait_ge(lg_done, h + 1)
                    nc.vector.tensor_tensor(logit[:, h, :], bank[4 + h % 4][:, 0:3 * P], amask, ALU.add
                                            ).then_inc(lg_out, 1)
                v.wait_ge(lg_out, 8)
                for t, (lo, n) in enumerate(((0, P), (P, S))):
                    nc.vector.tensor_reduce(mx[:, t, :], logit[:, :, lo:lo + n], AX.X, ALU.max).then_inc(v_chain, 1)
                    v.wait_ge(v_chain, c.up())
                    nc.vector.tensor_scalar(mx[:, t, :], mx[:, t, :], -1.0, None, ALU.mult).then_inc(max_ready, 1)
                v.wait_ge(consts, 11)
                for a in range(2):
                    v.wait_ge(tile_out, 16 + 4 * a)
                    nc.vector.tensor_tensor(u_sb[:, 2 * a:2 * a + 2, CW - 1:U], cy[:, 2 * a:2 * a + 2, :],
                                            cg[:, 2 * a:2 * a + 2, :], ALU.mult).then_inc(v_chain, 1)
                v.wait_ge(v_chain, c.up(2))
                for a in range(4):
                    nc.vector.tensor_scalar(cy[:, a, :], u_sb[:, a, 0:S], dw[:, a, 0:1], cv[:, 0, a:a + 1],
                                            ALU.mult, ALU.add).then_inc(v_chain, 1)
                c.up(4)
                base = c.n
                with v.Fori(1, CW) as j:
                    for a in range(4):
                        v.wait_ge(v_chain, base - 7 + a + j * 4)
                        nc.vector.scalar_tensor_tensor(cy[:, a, :], u_sb[:, a, bass.ds(j, S)], dw[:, a, bass.ds(j, 1)],
                                                       cy[:, a, :], ALU.mult, ALU.add).then_inc(v_chain, 1)
                v.wait_ge(v_chain, c.up(4 * (CW - 1)))
                nc.vector.sem_inc(conv_y, 1)
                v.wait_ge(exp_ready, 16)
                nc.vector.reciprocal(ssum[:, :, :], ssum[:, :, :]).then_inc(v_chain, 1)
                v.wait_ge(v_chain, c.up())
                for t, (lo, n) in enumerate(((0, P), (P, S))):
                    nc.vector.tensor_tensor(logit[:, :, lo:lo + n], logit[:, :, lo:lo + n],
                                            ssum[:, t, :].unsqueeze(2).to_broadcast([P, H, n]), ALU.mult
                                            ).then_inc(probs_ready, 1)
                v.wait_ge(mean_done, 1)
                nc.vector.tensor_scalar(mean, bank[7][:, 0:S], 1.0 / CC, None, ALU.mult).then_inc(v_chain, 1)
                v.wait_ge(v_chain, c.up())
                nc.vector.tensor_tensor(cy[:, :, :], cy[:, :, :], mean.unsqueeze(1).to_broadcast([P, 4, S]),
                                        ALU.subtract).then_inc(centred, 1)

                def merge(n):
                    v.wait_ge(y_done, n + 1)
                    b = bank[n % 4][:, 0:S]
                    if n < 8:
                        nc.vector.tensor_tensor(merged[:, n, :], b, sga[:, n, :], ALU.mult).then_inc(y_out, 1)
                    else:
                        m = n - 8
                        nc.vector.tensor_tensor(sgc[:, m, :], b, sgc[:, m, :], ALU.mult).then_inc(y_out, 1)
                        v.wait_ge(y_out, n + 1)
                        nc.vector.tensor_tensor(merged[:, m, :], merged[:, m, :], sgc[:, m, :], ALU.add
                                                ).then_inc(merged_ready, 1)
                v.wait_ge(std_ready, 1)
                nc.vector.reciprocal(std, std).then_inc(v_chain, 1)
                v.wait_ge(v_chain, c.up())
                nc.vector.tensor_tensor(cy[:, :, :], cy[:, :, :], std.unsqueeze(1).to_broadcast([P, 4, S]),
                                        ALU.mult).then_inc(v_chain, 1)
                v.wait_ge(v_chain, c.up())
                for a in range(4):
                    nc.vector.tensor_scalar(cy[:, a, :], cy[:, a, :], cv[:, 1, a:a + 1], cv[:, 2, a:a + 1],
                                            ALU.mult, ALU.add).then_inc(norm_ready, 1)
                for n in range(8):
                    merge(n)
                    if n == 3:
                        v.wait_ge(csig_ready, 1)
                        v.wait_ge(norm_ready, 4)
                        nc.vector.tensor_tensor(cy[:, :, :], cy[:, :, :], cg[:, :, :], ALU.mult).then_inc(conv_ready, 1)
                for n in range(8, 16):
                    merge(n)
                v.wait_ge(x_in, 16)
                for t in range(NT):
                    v.wait_ge(mix_done, 1 + 4 * t)
                    for j in range(2):
                        nc.vector.scalar_tensor_tensor(res[:, t, j * 512:(j + 1) * 512], x_sb[:, t, j * 512:(j + 1) * 512],
                                                       ALPHA, bank[4 + 2 * t + j][:, :], ALU.mult, ALU.add
                                                       ).then_inc(v_chain, 1)
                        v.wait_ge(v_chain, c.up())
                        nc.vector.bn_stats(stats[:, t, j, :], res[:, t, j * 512:(j + 1) * 512]).then_inc(v_chain, 1)
                        c.up()
                    v.wait_ge(v_chain, c.n)
                    nc.vector.bn_aggr(mv[:, t, :], stats[:, t, :, :]).then_inc(var1, 1)
                    v.wait_ge(std1, t + 1)
                    v.wait_ge(ln_in, 32)
                    nc.vector.reciprocal(rstd[:, t:t + 1], rstd[:, t:t + 1]).then_inc(v_chain, 1)
                    v.wait_ge(v_chain, c.up())
                    nc.vector.scalar_tensor_tensor(res[:, t, :], res[:, t, :], mv[:, t, 0:1], lng1,
                                                   ALU.subtract, ALU.mult).then_inc(v_chain, 1)
                    v.wait_ge(v_chain, c.up())
                    nc.vector.scalar_tensor_tensor(x1[:, t, :], res[:, t, :], rstd[:, t:t + 1], lnb1,
                                                   ALU.mult, ALU.add).then_inc(x1_ready, 1)
                for t in range(NT):
                    v.wait_ge(rl_done, t + 1)
                    nc.vector.tensor_tensor(rl[:, t, :], bank[4 + t][:, 0:NE], br, ALU.add).then_inc(v_chain, 1)
                    v.wait_ge(v_chain, c.up())
                    nc.vector.max(top8[:, t, :], rl[:, t, :]).then_inc(v_chain, 1)
                    v.wait_ge(v_chain, c.up())
                    nc.vector.max_index(idxu[:, t, :], top8[:, t, :], rl[:, t, :]).then_inc(v_chain, 1)
                    v.wait_ge(v_chain, c.up())
                    nc.vector.tensor_copy(idx8[:, t, :], idxu[:, t, :]).then_inc(v_chain, 1)
                    v.wait_ge(v_chain, c.up())
                    for r in range(TOPE):
                        nc.vector.scalar_tensor_tensor(mask[:, t, 0:NE], iota_e, idx8[:, t, r:r + 1],
                                                       mask[:, t, 0:NE], ALU.is_equal, ALU.add
                                                       ).then_inc(mask_ready if r == TOPE - 1 else v_chain, 1)
                        if r < TOPE - 1:
                            v.wait_ge(v_chain, c.up())
                    nc.vector.tensor_scalar(rl[:, t, :], rl[:, t, :], top8[:, t, 0:1], None, ALU.subtract
                                            ).then_inc(rl_shift, 1)
                v.wait_ge(rl_exp, 1)
                v.wait_ge(mask_ready, 2)
                nc.vector.tensor_tensor(gate[:, :, 0:NE], rl[:, :, :], mask[:, :, 0:NE], ALU.mult).then_inc(v_chain, 1)
                v.wait_ge(v_chain, c.up())
                nc.vector.tensor_reduce(rstd[:, 0:2], gate[:, :, 0:NE], AX.X, ALU.add).then_inc(v_chain, 1)
                v.wait_ge(v_chain, c.up())
                nc.vector.reciprocal(rstd[:, 0:2], rstd[:, 0:2]).then_inc(v_chain, 1)
                v.wait_ge(v_chain, c.up())
                nc.vector.tensor_tensor(gate[:, :, 0:NE], gate[:, :, 0:NE],
                                        rstd[:, 0:2].unsqueeze(2).to_broadcast([P, NT, NE]), ALU.mult
                                        ).then_inc(v_chain, 1)
                c.up()
                v.wait_ge(cum_done, 1)
                for t in range(NT):
                    nc.vector.scalar_tensor_tensor(slot1[:, t, 0:NE], bank[6][:, t * NE:(t + 1) * NE], 1.0,
                                                   mask[:, t, 0:NE], ALU.add, ALU.mult).then_inc(v_chain, 1)
                    c.up()
                nc.vector.tensor_scalar(wide_f, bank[6][0:1, 2 * NE:3 * NE], float(CAP), None, ALU.is_gt
                                        ).then_inc(wide_ready, 1)
                v.wait_ge(wide_ready, 1)
                nc.vector.tensor_copy(wide[:, :], wide_f).then_inc(wide_ready, 1)
                nc.vector.tensor_tensor(need, bank[7][0:MORE, 0:1], above, ALU.is_gt).then_inc(more_ready, 1)
                v.wait_ge(more_ready, 1)
                v.wait_ge(rank_done, 1)
                nc.vector.tensor_scalar(place, iota_e[0:MORE, 0:LIST], bank[4][0:MORE, 0:1], need, ALU.is_equal, ALU.mult
                                        ).then_inc(more_ready, 1)
                v.wait_ge(list_done, 1)
                nc.vector.tensor_copy(more[:, :], bank[5][0:1, 0:LIST + 1])


        def gather(pe):
            for k in range(KD):
                for t in range(NT):
                    mm = pe.matmul(bank[4 + k // 4][:, (k % 4) * P:(k % 4 + 1) * P], x1[:, t, k * P:(k + 1) * P],
                                   sel[:, t, :, :], start=(t == 0), stop=(t == NT - 1))
            return mm

        def gate_up(pe, w, k, q, done=None):
            a = (k % 2) * CAP
            for n in BANK_ORDER:
                mm = pe.matmul(bank[n][a:a + CAP, :], XT[:, k, q, :], w[:, n * 512:(n + 1) * 512],
                               start=(k < 2), stop=(k >= KD - 2))
                if k == KD - 1:
                    mm.then_inc(done, 1)
            return mm

        def gather_wide(pe):
            for k in range(KD):
                for t in range(NT):
                    mm = pe.matmul(bank[4 + k // 4][:, (k % 4) * P:(k % 4 + 1) * P], x1[:, t, k * P:(k + 1) * P],
                                   sel_w[:, t, :], start=(t == 0), stop=(t == NT - 1))
            return mm

        def gate_up_wide(pe, w, k, done):
            for n in BANK_ORDER:
                mm = pe.matmul(bank[n][:, :], XT_w[:, k, :], w[:, n * 512:(n + 1) * 512],
                               start=(k == 0), stop=(k == KD - 1))
                if k == KD - 1:
                    mm.then_inc(done, 1)
            return mm

        def down_wide(pe, w, f, kk):
            for n in range(2):
                mm = pe.matmul(bank[6 + n][:, :], act_w[:, f, :], w[:, kk * 1024 + n * 512:kk * 1024 + (n + 1) * 512],
                               start=(f == 0), stop=(f == 7))
            return mm

        def turn(pe, hh):
            for g in range(2):
                for f in range(4):
                    at = g * 1024 + (4 * hh + f) * P
                    mm = pe.transpose(bank[4 + 2 * hh + g][:, f * P:(f + 1) * P], hsb[:, at:at + P], ident)
            return mm

        def down(pe, w, f, kk):
            a = (f % 2) * CAP
            for n in range(2):
                mm = pe.matmul(bank[6 + n][a:a + CAP, :], act_sb[:, f, :], w[:, kk * 1024 + n * 512:kk * 1024 + (n + 1) * 512],
                               start=(f < 2), stop=(f >= 6))
            return mm

        def combine(pe, q, j):
            return pe.matmul(bank[j][:, :], G2[:, q, (j // 2) * P:(j // 2 + 1) * P],
                             ysb[:, (j % 2) * 512:(j % 2) * 512 + 512], start=True, stop=True)

        def acc_part(j):
            return acc[:, j // 2, (j % 2) * 512:(j % 2) * 512 + 512]

        def halves(b):
            return bank[b][:, :].rearrange("p (f h c) -> p f h c", f=4, h=2)


        def swiglu(v, e, hh, n):
            fs = slice(4 * hh, 4 * hh + 4)
            for g, dst in enumerate((gt, up)):
                v.wait_ge(t_done, n)
                src_ = halves(4 + 2 * hh + g)
                nc.vector.tensor_tensor(dst[:, fs, :], src_[:, :, 0, :],
                                        bgu_of(e, g, hh).to_broadcast([P, 4, CAP]), ALU.add).then_inc(sw_biased, 1)
                v.wait_ge(sw_biased, n * 2 - 1 + g)
                nc.vector.tensor_tensor(dst[:, fs, :], src_[:, :, 1, :], dst[:, fs, :], ALU.add
                                        ).then_inc(sw_summed, 1)
            v.wait_ge(sw_summed, n * 2 - 1)
            nc.vector.tensor_scalar(gt[:, fs, :], gt[:, fs, :], LIMIT, None, ALU.min).then_inc(sig_in, 1)
            v.wait_ge(sw_summed, n * 2)
            nc.vector.tensor_scalar(up[:, fs, :], up[:, fs, :], LIMIT, -LIMIT, ALU.min, ALU.max).then_inc(t_read, 1)
            v.wait_ge(t_read, n)
            v.wait_ge(sig_in, n)
            nc.vector.scalar_tensor_tensor(up[:, fs, :], up[:, fs, :], 1.0, gt[:, fs, :], ALU.add, ALU.mult
                                           ).then_inc(sw_prod, 1)
            v.wait_ge(sw_prod, n)
            v.wait_ge(sig_out, n)
            nc.vector.tensor_tensor(act_sb[:, fs, :], up[:, fs, :], sg[:, fs, :], ALU.mult).then_inc(act_ready, 1)

        def swiglu_wide(v, e, hh, n):
            if hh == 1:
                v.wait_ge(act_ready, n - 1)
            for g, dst in enumerate((gt_w, up_w)):
                v.wait_ge(t_done, n)
                nc.vector.tensor_tensor(dst, bank[4 + 2 * hh + g][:, :].rearrange("p (f c) -> p f c", f=4),
                                        bgu_of(e, g, hh).to_broadcast([P, 4, WIDE]), ALU.add).then_inc(sw_biased, 1)
            v.wait_ge(sw_biased, n * 2)
            nc.vector.sem_inc(sw_summed, 2)
            nc.vector.tensor_scalar(gt_w, gt_w, LIMIT, None, ALU.min).then_inc(sig_in, 1)
            nc.vector.tensor_scalar(up_w, up_w, LIMIT, -LIMIT, ALU.min, ALU.max).then_inc(t_read, 1)
            v.wait_ge(t_read, n)
            v.wait_ge(sig_in, n)
            nc.vector.scalar_tensor_tensor(up_w, up_w, 1.0, gt_w, ALU.add, ALU.mult).then_inc(sw_prod, 1)
            v.wait_ge(sw_prod, n)
            v.wait_ge(sig_out, n)
            nc.vector.tensor_tensor(act_w[:, 4 * hh:4 * hh + 4, :], up_w, sg_w, ALU.mult).then_inc(act_ready, 1)

        def bgu_of(e, g, hh):
            at = g * 8 + 4 * hh
            return bgu[:, bass.ds(e, 1), at:at + 4].rearrange("p e f -> p (e f)").unsqueeze(2)

        def select_wide(v, e, q):
            nc.vector.tensor_tensor(sel_w, iota_c.unsqueeze(1).to_broadcast([P, NT, WIDE]),
                                    slot1[:, :, bass.ds(e, 1)].to_broadcast([P, NT, WIDE]),
                                    ALU.is_equal).then_inc(selw_onehot, 1)
            v.wait_ge(selw_onehot, e + 1)
            nc.vector.tensor_scalar(slot1[:, :, bass.ds(e, 1)], slot1[:, :, bass.ds(e, 1)], float(CAP),
                                    None, ALU.subtract).then_inc(slot_moved, 1)
            for t in range(NT):
                nc.vector.tensor_scalar(selg[:, q, t, :, :].rearrange("p h c -> p (h c)"), sel_w[:, t, :],
                                        gate[:, t, bass.ds(e, 1)], None, ALU.mult
                                        ).then_inc(selw_ready if t == NT - 1 else selg_part, 1)

        def select(v, first, n0):
            nc.vector.tensor_tensor(sel[:, :, :, :],
                                    iota_c[:, 0:CAP].unsqueeze(1).unsqueeze(1).to_broadcast([P, NT, 2, CAP]),
                                    slot1[:, :, bass.ds(first, 2)].unsqueeze(3).to_broadcast([P, NT, 2, CAP]),
                                    ALU.is_equal).then_inc(sel_ready, 1)
            v.wait_ge(sel_ready, n0)
            for q in range(2):
                for t in range(NT):
                    nc.vector.tensor_tensor(
                        selg[:, q, t, :, :], sel[:, t, q:q + 1, :].to_broadcast([P, 2, CAP]),
                        gate[:, t, bass.ds(first + q, 1)].unsqueeze(2).to_broadcast([P, 2, CAP]),
                        ALU.mult).then_inc(selg_ready if (q, t) == (1, 1) else selg_part, 1)

        with nc.Block() as block:
            @block.sync
            def _(sp):
                def load(e, q, c):
                    back = ES - CPE
                    sp.wait_ge(*(expert_used(e - 1, c - back) if c >= back else expert_used(e - 2, c - back + CPE)))
                    load_expert(sp, e, q, c)

                for e in range(1, UNROLL):
                    for c in range(ES - CPE if e == 1 else 0, CPE):
                        load(e, e, c)
                with sp.Fori(1, NE // UNROLL) as i:
                    for q in range(UNROLL):
                        for c in range(CPE):
                            load(i * UNROLL + q, q, c)
                for j in range(4):
                    sp.wait_ge(*expert_used(NE - 2, CPE - 4 + j))
                    sp.dma_start(expert_w(0, j).rearrange("p (k c) -> p k c", k=KD),
                                 w_pg[:, j * 256:(j + 1) * 256].rearrange("(k p) c -> p k c", p=P)
                                 ).then_inc(e_in[j], 16)
                n_more = sp.value_load(more[0:1, LIST:LIST + 1], min_val=0, max_val=LIST)
                with sp.If(n_more > 0):
                    with sp.Fori(0, n_more) as r:
                        e = sp.value_load(more[0:1, bass.ds(r, 1)], min_val=0, max_val=NE - 1)
                        for c in range(CPE):
                            sp.wait_ge(*expert_used(r + (NE - 1), c))
                            load_expert(sp, e, UNROLL - 1, c)

            @block.gpsimd
            def _(g):
                g.memset(ysb, 0.0).then_inc(first_zero, 1)
                g.memset(G2[:, 1, :], 0.0).then_inc(first_zero, 1)
                g.wait_ge(first_zero, 2)
                g.dma_start(ysb[0:NE, :], b_dn).then_inc(first_rows, 16)
                g.wait_ge(first_rows, 16)
                g.sem_inc(y_sb_out, 1)

            @block.tensor
            def _(pe):
                def first_half(e, q, chunk, wide_e):
                    with pe.If(wide_e > 0):
                        pe.wait_ge(selw_ready, e + 1)
                        gather_wide(pe).then_inc(gathw_done, 1)
                        pe.wait_ge(xtw_ready, e + 1)
                    with pe.Else():
                        pe.sem_inc(gathw_done, 1)
                    for t in range(NT):
                        mm = pe.transpose(bank[4][:, t * P:(t + 1) * P],
                                          selg[:, q % 2, t, :, :].rearrange("p h c -> p (h c)"), ident)
                    mm.then_inc(sgt_done, 1)
                    pe.wait_ge(acc_out, e * 4 + 4)
                    with pe.If(wide_e > 0):
                        for k in range(KD):
                            mm = gate_up_wide(pe, chunk(k), k, gu_done)
                            if k < KD - 1:
                                mm.then_inc(chunk_used, 1)
                    with pe.Else():
                        for k in range(KD):
                            mm = gate_up(pe, chunk(k), k, q % 2, gu_done)
                            if k < KD - 1:
                                mm.then_inc(chunk_used, 1)
                    pe.wait_ge(g2_out, e + 2)
                    for hh in range(2):
                        pe.wait_ge(h_out, e * 4 + (2 + 2 * hh))
                        turn(pe, hh).then_inc(t_done, 1)

                def rows_in(e, q):
                    pe.wait_ge(y_sb_out, e + 1)
                    for j in range(4):
                        combine(pe, 1 - q % 2, j).then_inc(comb_done, 1)

                def second_half(e, chunk, product=down):
                    pe.wait_ge(t_read, e * 2 + 2)
                    for f in range(8):
                        if f % 4 == 0:
                            pe.wait_ge(act_ready, e * 2 + (f // 4 + 1))
                        if f % 2 == 0:
                            w = chunk(KD + f // 2)
                        mm = product(pe, w, f, f % 2)
                        if f % 2 == 1 and f < 7:
                            mm.then_inc(chunk_used, 1)
                    mm.then_inc(d_done, 1)

                pe.wait_ge(selg_ready, 1)
                gather(pe).then_inc(gath_done, 1)
                for t in range(NT):
                    mm = pe.transpose(bank[6][0:NE, t * P:(t + 1) * P], gate[:, t, 0:NE], ident)
                mm.then_inc(gT_done, 1)
                with pe.Fori(0, NE // UNROLL) as i:
                    for q in range(UNROLL):
                        e = i * UNROLL + q
                        pair = i * (UNROLL // 2) + q // 2
                        if q % 2 == 0:
                            pe.wait_ge(xt_ready, pair + 1)
                            pe.wait_ge(selg_ready, pair + 1)

                        def chunk(c):
                            pe.wait_ge(*expert_in(i, q, c))
                            return expert_w(q, c)

                        wide_e = pe.value_load(wide[0:1, bass.ds(e, 1)], min_val=0, max_val=1)
                        first_half(e, q, chunk, wide_e)
                        rows_in(e, q)
                        if q % 2 == 1:
                            pe.wait_ge(selg_ready, pair + 2)
                            pe.wait_ge(t_read, e * 2 + 1)
                            gather(pe).then_inc(gath_done, 1)
                        with pe.If(wide_e > 0):
                            second_half(e, chunk, down_wide)
                        with pe.Else():
                            second_half(e, chunk)
                n_more = pe.value_load(more[0:1, LIST:LIST + 1], min_val=0, max_val=LIST)
                with pe.If(n_more > 0):
                    with pe.Fori(0, n_more) as r:
                        e = r + NE

                        def chunk(c):
                            i = (UNROLL - 1) * CPE + c
                            pe.wait_ge(e_in[i % ES], r * 16 + (16 * NE * CPE // ES + 16))
                            return expert_w(UNROLL - 1, c)

                        pe.wait_ge(y_sb_out, e + 1)
                        pe.wait_ge(h_out, e * 4)
                        pe.wait_ge(acc_out, e * 4 + 4)
                        for j in range(4):
                            combine(pe, 1, j).then_inc(comb_done, 1)
                        pe.wait_ge(selg_ready, r + (NE // 2 + 2))
                        pe.wait_ge(xt_ready, r + (NE // 2 + 1))
                        gather(pe).then_inc(gath_done, 1)
                        pe.wait_ge(xt_ready, r + (NE // 2 + 2))
                        for t in range(NT):
                            mm = pe.transpose(bank[4][:, t * P:(t + 1) * P],
                                              selg[:, 0, t, :, :].rearrange("p h c -> p (h c)"), ident)
                        mm.then_inc(sgt_done, 1)
                        pe.wait_ge(acc_out, e * 4 + 8)
                        for k in range(KD):
                            mm = gate_up(pe, chunk(k), k, 0, gu_done)
                            if k < KD - 1:
                                mm.then_inc(chunk_used, 1)
                        pe.wait_ge(g2_out, e + 2)
                        for hh in range(2):
                            pe.wait_ge(h_out, e * 4 + (2 + 2 * hh))
                            turn(pe, hh).then_inc(t_done, 1)
                        second_half(e, chunk)
                with pe.If(n_more > 0):
                    pe.wait_ge(y_sb_out, n_more + (NE + 1))
                    pe.wait_ge(acc_out, n_more * 4 + (4 * NE + 4))
                with pe.Else():
                    pe.wait_ge(y_sb_out, NE + 1)
                    pe.wait_ge(acc_out, 4 * NE + 4)
                for j in range(4):
                    combine(pe, 1, j).then_inc(comb_done, 1)

            @block.scalar
            def _(a):
                def xt_out(n):
                    a.wait_ge(gath_done, n)
                    for b in range(2):
                        a.activation(XT[:, 4 * b:4 * b + 4, :, :],
                                     bank[4 + b][:, :].rearrange("p (k q c) -> p k q c", k=4, q=2),
                                     ACT.Identity).then_inc(xt_half if b == 0 else xt_ready, 1)

                def gates_out(e, q):
                    a.wait_ge(sgt_done, e + 1)
                    a.activation(G2[:, q, :], bank[4][:, 0:S], ACT.Identity).then_inc(g2_out, 1)

                def sums_out(e):
                    for n, b in enumerate(BANK_ORDER):
                        a.wait_ge(gu_done, e * 4 + (n + 1))
                        a.activation(hsb[:, b * 512:(b + 1) * 512], bank[b][:, :], ACT.Identity).then_inc(h_out, 1)

                def sigmoids_wide(e):
                    for hh in range(2):
                        a.wait_ge(sig_in, e * 2 + (hh + 1))
                        a.activation(sg_w, gt_w, ACT.Sigmoid, scale=SW_ALPHA).then_inc(sig_out, 1)

                def sigmoids(e):
                    for hh in range(2):
                        a.wait_ge(sig_in, e * 2 + (hh + 1))
                        a.activation(sg[:, 4 * hh:4 * hh + 4, :], gt[:, 4 * hh:4 * hh + 4, :], ACT.Sigmoid,
                                     scale=SW_ALPHA).then_inc(sig_out, 1)

                def rows_out(e):
                    a.wait_ge(d_done, e + 1)
                    for n in range(2):
                        a.activation(ysb[:, n * 512:(n + 1) * 512], bank[6 + n][:, :], ACT.Identity
                                     ).then_inc(y_half if n == 0 else y_sb_out, 1)

                xt_out(1)
                a.wait_ge(gT_done, 1)
                a.wait_ge(first_zero, 2)
                a.activation(G2[0:NE, 1, :], bank[6][0:NE, 0:S], ACT.Identity).then_inc(g2_out, 1)
                with a.Fori(0, NE // UNROLL) as i:
                    for q in range(UNROLL):
                        e = i * UNROLL + q
                        wide_e = a.value_load(wide[0:1, bass.ds(e, 1)], min_val=0, max_val=1)
                        with a.If(wide_e > 0):
                            a.wait_ge(gathw_done, e + 1)
                            for b in range(2):
                                a.activation(XT_w[:, 4 * b:4 * b + 4, :], bank[4 + b][:, :].rearrange("p (k c) -> p k c", k=4),
                                             ACT.Identity).then_inc(xt_half if b == 0 else xtw_ready, 1)
                        with a.Else():
                            a.sem_inc(xtw_ready, 1)
                        gates_out(e, q % 2)
                        sums_out(e)
                        with a.If(wide_e > 0):
                            sigmoids_wide(e)
                        with a.Else():
                            sigmoids(e)
                        if q % 2 == 1:
                            xt_out(i * (UNROLL // 2) + (q // 2 + 2))
                        rows_out(e)
                n_more = a.value_load(more[0:1, LIST:LIST + 1], min_val=0, max_val=LIST)
                with a.If(n_more > 0):
                    with a.Fori(0, n_more) as r:
                        xt_out(r + (NE // 2 + 2))
                        gates_out(r + NE, 1)
                        sums_out(r + NE)
                        sigmoids(r + NE)
                        rows_out(r + NE)

            @block.vector
            def _(v):
                def add_rows(n):
                    for j in range(4):
                        v.wait_ge(comb_done, n + (j + 1))
                        v.wait_ge(acc_out, n + (j + 1))
                        nc.vector.tensor_tensor(acc_part(j), bank[j][:, :], acc_part(j), ALU.add).then_inc(acc_out, 1)

                select(v, 0, 1)
                for j in range(4):
                    nc.vector.tensor_scalar(acc_part(j), x1[:, j // 2, (j % 2) * 512:(j % 2) * 512 + 512], ALPHA,
                                            None, ALU.mult).then_inc(acc_out, 1)
                with v.Fori(0, NE // UNROLL) as i:
                    for q in range(UNROLL):
                        e = i * UNROLL + q
                        wide_e = v.value_load(wide[0:1, bass.ds(e, 1)], min_val=0, max_val=1)
                        with v.If(wide_e > 0):
                            v.wait_ge(gath_done, i * (UNROLL // 2) + (q // 2 + 1))
                            select_wide(v, e, q % 2)
                        with v.Else():
                            nc.vector.sem_inc(selw_onehot, 1)
                            nc.vector.sem_inc(slot_moved, 1)
                            nc.vector.sem_inc(selw_ready, 1)
                        if q % 2 == 1:
                            v.wait_ge(sgt_done, e + 1)
                            select(v, e + 1, i * (UNROLL // 2) + (q // 2 + 2))
                        with v.If(wide_e > 0):
                            for hh in range(2):
                                swiglu_wide(v, e, hh, e * 2 + (hh + 1))
                        with v.Else():
                            for hh in range(2):
                                swiglu(v, e, hh, e * 2 + (hh + 1))
                        add_rows(e * 4)
                n_more = v.value_load(more[0:1, LIST:LIST + 1], min_val=0, max_val=LIST)
                with v.If(n_more > 0):
                    with v.Fori(0, n_more) as r:
                        e = v.value_load(more[0:1, bass.ds(r, 1)], min_val=0, max_val=NE - 1)
                        v.wait_ge(gath_done, r + (NE // 2 + 1))
                        v.wait_ge(slot_moved, r + NE)
                        nc.vector.tensor_scalar(slot1[:, :, bass.ds(e, 1)], slot1[:, :, bass.ds(e, 1)], float(CAP),
                                                None, ALU.subtract).then_inc(slot_moved, 1)
                        v.wait_ge(slot_moved, r + (NE + 1))
                        select(v, e, r + (NE // 2 + 2))
                        add_rows(r * 4 + 4 * NE)
                        for hh in range(2):
                            swiglu(v, e, hh, r * 2 + (2 * NE + hh + 1))
                with v.If(n_more > 0):
                    add_rows(n_more * 4 + 4 * NE)
                with v.Else():
                    add_rows(4 * NE)

        with nc.Block() as block:
            @block.tensor
            def _(pe):
                for t in range(NT):
                    for k in range(KD):
                        mm = pe.transpose(bank[2 * t + k // 4][:, (k % 4) * P:(k % 4 + 1) * P],
                                          acc[:, t, k * P:(k + 1) * P], ident)
                        if k % 4 == 3:
                            mm.then_inc(hT_done, 1)
                for t in range(NT):
                    pe.wait_ge(hT_out, 2 * t + 2)
                    for j in range(4):
                        if t == 0:
                            pe.wait_ge(e_in[j], 16 * (NE * CPE // ES + 1))
                        w = expert_w(0, j).rearrange("p (k c) -> p k c", k=KD)
                        for k in range(KD):
                            mm = pe.matmul(bank[4 + 2 * t + j // 2][:, (j % 2) * 256:(j % 2) * 256 + 256],
                                           hT[:, k, t * P:(t + 1) * P], w[:, k, :], start=(k == 0), stop=(k == KD - 1))
                        if j % 2 == 1:
                            mm.then_inc(pg_done, 1)

            @block.scalar
            def _(a):
                a.dma_start(lng2, ln2g.partition_broadcast(P)).then_inc(ln_in, 16)
                a.dma_start(lnb2, ln2b.partition_broadcast(P)).then_inc(ln_in, 16)
                for n in range(4):
                    a.wait_ge(hT_done, n + 1)
                    a.activation(hT[:, 4 * (n % 2):4 * (n % 2) + 4, (n // 2) * P:(n // 2 + 1) * P],
                                 bank[n][:, :].rearrange("p (k t) -> p k t", k=4), ACT.Identity).then_inc(hT_out, 1)
                for n in range(4):
                    a.wait_ge(pg_done, n + 1)
                    a.activation(pge[:, n // 2, (n % 2) * 512:(n % 2) * 512 + 512], bank[4 + n][:, :], ACT.Sigmoid
                                 ).then_inc(pge_ready, 1)
                for t in range(NT):
                    a.wait_ge(var2, t + 1)
                    a.activation(rstd[:, t:t + 1], mv[:, t, 1:2], ACT.Sqrt, bias=epsc).then_inc(std2, 1)

            @block.vector
            def _(v):
                c = Tally()
                for t in range(NT):
                    for j in range(2):
                        at = slice(j * 512, (j + 1) * 512)
                        v.wait_ge(pge_ready, 2 * t + j + 1)
                        nc.vector.tensor_tensor(pge[:, t, at], pge[:, t, at], pple[:, t, at], ALU.mult).then_inc(t_chain, 1)
                        v.wait_ge(t_chain, c.up())
                        nc.vector.tensor_tensor(pge[:, t, at], pge[:, t, at], acc[:, t, at], ALU.add).then_inc(t_chain, 1)
                        v.wait_ge(t_chain, c.up())
                        nc.vector.bn_stats(stats[:, t, j, :], pge[:, t, at]).then_inc(t_chain, 1)
                        v.wait_ge(t_chain, c.up())
                    nc.vector.bn_aggr(mv[:, t, :], stats[:, t, :, :]).then_inc(var2, 1)
                    v.wait_ge(std2, t + 1)
                    nc.vector.reciprocal(rstd[:, t:t + 1], rstd[:, t:t + 1]).then_inc(t_chain, 1)
                    v.wait_ge(t_chain, c.up())
                    v.wait_ge(ln_in, 64)
                    nc.vector.scalar_tensor_tensor(pge[:, t, :], pge[:, t, :], mv[:, t, 0:1], lng2,
                                                   ALU.subtract, ALU.mult).then_inc(t_chain, 1)
                    v.wait_ge(t_chain, c.up())
                    nc.vector.scalar_tensor_tensor(pge[:, t, :], pge[:, t, :], rstd[:, t:t + 1], lnb2,
                                                   ALU.mult, ALU.add).then_inc(out_ready, 1)

            @block.sync
            def _(sp):
                for t in range(NT):
                    sp.wait_ge(out_ready, t + 1)
                    sp.dma_start(out[t * P:(t + 1) * P, :], pge[:, t, :]).then_inc(out_done, 16)
                sp.wait_ge(out_done, 32)


_INS = ["x", "xT", "pT", "w_in", "bT", "bki", "b_in", "w_oa", "w_oc", "w_out", "dwT", "convT", "ln1g", "ln1b", "w_r",
        "b_r", "w_gu", "bguT", "w_dn", "b_dn", "w_pg", "w_pp", "ln2g", "ln2b", "relb", "onehot", "passes"]


def kernel(x, p, w_in, b_in, w_o_attn, w_dw, b_dw, conv_ln_g, conv_ln_b, w_o_conv, w_out, ln1_g, ln1_b,
           w_router, b_router, w_gate_up, b_gate_up, w_down, b_down, w_ple_gate, w_ple_proj, ln2_g, ln2_b, rel_bias):
    import numpy as _np
    import concourse.bacc as _bacc
    from concourse import mybir as _mybir
    from concourse.bass_utils import run_bass_kernel_spmd as _run

    def rows(a):
        return _np.asarray(a).reshape(-1, P).T

    b = _np.asarray(b_in[0])
    placed = [b[c:c + n] for c, n in ((QI0, 512), (Q0, 512), (K0, 512), (CA0, 512), (CG0, 512), (GA0, D), (GC0, D))]
    given = {
        "x": x[0], "xT": _np.asarray(x[0]).T, "pT": _np.asarray(p[0, 0]).T, "w_in": w_in[0],
        "bT": _np.concatenate([rows(a) for a in placed], axis=1),
        "bki": _np.concatenate([b[KI0:WI0], b[KI0:WI0]])[:, None], "b_in": b,
        "w_oa": w_o_attn[0], "w_oc": w_o_conv[0], "w_out": w_out[0],
        "dwT": _np.asarray(w_dw[0]).T.reshape(4, P, CW).transpose(1, 0, 2).reshape(P, 4 * CW),
        "convT": _np.concatenate([rows(a[0]) for a in (b_dw, conv_ln_g, conv_ln_b)], axis=1),
        "ln1g": ln1_g[0], "ln1b": ln1_b[0], "w_r": w_router[0], "b_r": b_router[0],
        "w_gu": w_gate_up[0], "bguT": rows(_np.asarray(b_gate_up[0]).reshape(-1)), "w_dn": w_down[0],
        "b_dn": b_down[0], "w_pg": w_ple_gate[0], "w_pp": w_ple_proj[0], "ln2g": ln2_g[0], "ln2b": ln2_b[0],
        "relb": rel_bias, "onehot": rel_bucket_onehot(),
        "passes": further_passes(),
    }
    nc = _bacc.Bacc("TRN2", target_bir_lowering=False, num_devices=1)
    arrays, args = {}, []
    for name in _INS:
        a = _np.ascontiguousarray(given[name])
        arrays[f"in_{name}"] = a
        args.append(nc.dram_tensor(f"in_{name}", a.shape, _mybir.dt.from_np(a.dtype), kind="ExternalInput").ap())
    out = nc.dram_tensor("out_0", (S, D), _mybir.dt.float32, kind="ExternalOutput").ap()
    table = nc.dram_tensor("bias_table", (H, S + P), _mybir.dt.float32, kind="Internal").ap()
    program(nc, *args, out, table)
    r = _run(nc, [arrays], core_ids=[0])
    return r.results[0]["out_0"].reshape(1, S, D)
```

```python
import concourse.bass as bass
from concourse import mybir
from contextlib import ExitStack
import math
import numpy as np

D, S, P = 1024, 256, 128
NT = S // P
KD = D // P
H, HD = 8, 64
TOPK = min(256, S // 4)
IDX_SCALE = (8 ** -0.5) * (64 ** -0.5)
CW, CC = 31, 512
TAPS = 6
assert (CW - 1) % TAPS == 0
NB = 32
NE, TOPE = 32, 4
PD = 256
CAP = 64
WIDE = 2 * CAP
LIMIT, SW_ALPHA = 7.0, 1.702
EPS = 1e-5
ALPHA = 2 ** 0.25
NEG = -1.0e30
BELOW = -3.0e38
TAKEN = -3.4e38

NMORE = (S - WIDE) // CAP
MORE = NMORE * NE
LIST = NT * P * TOPE // CAP

Q0, K0, V0, QI0 = 0, 512, 1024, 1536
KI0, WI0, CA0, CG0, GA0, GC0, IN_COLS = 2048, 2112, 2120, 2632, 3144, 4168, 5192

NS = 12
ES = 16
SLOT = 2048
FRONT = ([("in", QI0, 256), ("in", QI0 + 256, 256), ("in", KI0, 72)]
         + [("in", c, 256) for c in (Q0, Q0 + 256, K0, K0 + 256, V0, V0 + 256)]
         + [("in", c, 256) for c in (CA0, CG0, CA0 + 256, CG0 + 256)]
         + [("in", GA0 + 256 * j, 256) for j in range(4)] + [("in", GC0 + 256 * j, 256) for j in range(4)]
         + [("oa", 0, 512), ("oa", 512, 512), ("oc", 0, 512), ("oc", 512, 512)]
         + [("out", 256 * j, 256) for j in range(4)])
NF = len(FRONT)
CPE = 12
UNROLL = 4
assert UNROLL * CPE % ES == 0


def rel_bucket_onehot():
    dist = (S - 1) - np.arange(S + P)
    d = np.maximum(dist, 1).astype(np.float32)
    large = 16 + (np.log(d / np.float32(16)) / np.float32(math.log(128 / 16)) * np.float32(16)).astype(np.int32)
    bucket = np.where(dist < 16, dist, np.minimum(large, NB - 1))
    return ((bucket[None, :] == np.arange(NB)[:, None]) & (dist >= 0)[None, :]).astype(np.float32)


EMBED_BANK = (4, 6, 0, 1)
ROUTE_BANK = (5, 7)
ROW_ORDER = (0, 2, 1, 3)
BANK_ORDER = (0, 2, 1, 3)


def further_passes():
    taken, expert = np.repeat(WIDE + CAP * np.arange(NMORE), NE), np.tile(np.arange(NE), NMORE)
    return np.stack([taken, expert], axis=1).astype(np.float32)


class Tally:

    def __init__(self, start=0):
        self.n = start

    def up(self, k=1):
        self.n += k
        return self.n


def program(nc, x, xT, pT, w_in, bT, bki, b_in, w_oa, w_oc, w_out, dwT, convT, ln1g, ln1b, w_r, b_r,
            w_gu, bguT, w_dn, b_dn, w_pg, w_pp, ln2g, ln2b, relb, onehot, passes, out, table):
    F32, I32, U32 = mybir.dt.float32, mybir.dt.int32, mybir.dt.uint32
    ALU, ACT, AX = mybir.AluOpType, mybir.ActivationFunctionType, mybir.AxisListType
    ctx = ExitStack()
    with ctx:
        def sb(name, shape, dt=F32):
            return ctx.enter_context(nc.sbuf_tensor(name, shape, dt))

        def sem(name):
            return ctx.enter_context(nc.semaphore(name))

        ring = sb("ring", [P, NS, SLOT])
        arena = sb("arena", [P, 27400])
        bank = [ctx.enter_context(nc.psum_tensor(f"bank{i}", [P, 512], F32)) for i in range(8)]

        def view(at, n):
            return arena[:, at:at + n]

        x1 = view(0, 2048).rearrange("p (t d) -> p t d", t=NT)
        acc = view(2048, 2048).rearrange("p (t d) -> p t d", t=NT)
        pple = view(4096, 2048).rearrange("p (t d) -> p t d", t=NT)
        xT_sb = view(4096, 2048).rearrange("p (k t) -> p k t", k=KD)
        x_sb = x1
        qT = view(6144, 1024).rearrange("p (a t) -> p a t", a=4)
        kT = view(7168, 1024).rearrange("p (a t) -> p a t", a=4)
        qiT = view(8192, 1024).rearrange("p (a t) -> p a t", a=4)
        kiT = view(9216, 256)
        v_sb = view(9472, 1024).rearrange("p (t c) -> p t c", t=NT)
        U = CW - 1 + S
        u_sb = view(10496, 4 * U).rearrange("p (a t) -> p a t", a=4)
        cy = view(11640, 1024).rearrange("p (a t) -> p a t", a=4)
        cg = view(12664, 1024).rearrange("p (a t) -> p a t", a=4)
        sga = view(13688, 2048).rearrange("p (a t) -> p a t", a=KD)
        sgc = view(15736, 2048).rearrange("p (a t) -> p a t", a=KD)
        logit = view(17784, 3072).rearrange("p (h s) -> p h s", h=H)
        hankel = view(20856, 2048).rearrange("p (h s) -> p h s", h=H)
        score = view(22904, 384)
        rest = view(23288, 384)
        amask = view(23672, 384)
        relu = view(24056, 768).rearrange("p (b s) -> p b s", b=2)
        pT_h = view(24056, 768).rearrange("p (b s) -> p b s", b=2)
        attnT = view(8192, 1024).rearrange("p (a t) -> p a t", a=4)
        merged = acc.rearrange("p t d -> p (t d)").rearrange("p (a t) -> p a t", a=KD)
        lng1 = view(19832, 1024)
        lnb1 = view(12664, 1024)
        extra = [view(at, SLOT) for at in (13688, 15736, 17784, 20856)]
        res = view(6144, 2048).rearrange("p (t d) -> p t d", t=NT)
        x1T = view(8192, 2048).rearrange("p (k t) -> p k t", k=KD)
        mean = view(9216, 256)
        std = view(22904, 256)
        o = 6144
        XT = view(o, 1024).rearrange("p (k q c) -> p k q c", k=KD, q=2)
        hsb = view(o + 1024, 2048)
        gt = view(o + 3072, 512).rearrange("p (f c) -> p f c", f=8)
        up = view(o + 3584, 512).rearrange("p (f c) -> p f c", f=8)
        sg = view(o + 4096, 512).rearrange("p (f c) -> p f c", f=8)
        act_sb = view(o + 4608, 512).rearrange("p (f c) -> p f c", f=8)
        ysb = view(o + 5120, 1024)
        G2 = view(o + 6144, 512).rearrange("p (q t) -> p q t", q=2)
        sel = view(o + 6656, 256).rearrange("p (t q c) -> p t q c", t=NT, q=2)
        XT_w = view(19832, 1024).rearrange("p (k c) -> p k c", k=KD)
        act_w = view(22904, 1024).rearrange("p (f c) -> p f c", f=8)
        gt_w, up_w, sg_w = (view(o + at, 512).rearrange("p (f c) -> p f c", f=4) for at in (3072, 3584, 4096))
        sel_w = view(o + 6656, 256).rearrange("p (t c) -> p t c", t=NT)
        hT = view(13688, 2048).rearrange("p (k t) -> p k t", k=KD)
        pge = view(15736, 2048).rearrange("p (t d) -> p t d", t=NT)
        lng2, lnb2 = view(7168, 1024), view(8192, 1024)
        o = 24824
        ident, flip, upper, ones = (view(o + P * j, P) for j in range(4))
        o += 512
        iota_e = view(o + 64, NE)
        bT_sb = view(o + 96, 36)
        bq = view(o + 132, 4)
        bki_sb = view(o + 136, 1)
        dw = view(o + 137, 124).rearrange("p (a j) -> p a j", a=4)
        cv = view(o + 261, 12).rearrange("p (j a) -> p j a", j=3)
        wsc = view(o + 273, 16).rearrange("p (t h) -> p t h", t=NT)
        bwi = view(o + 289, 8)
        top8 = view(o + 297, 16).rearrange("p (t h) -> p t h", t=NT)
        idx8 = view(o + 313, 16).rearrange("p (t h) -> p t h", t=NT)
        stats = view(o + 329, 24).rearrange("p (t a b) -> p t a b", t=NT, a=2)
        mv = view(o + 353, 4).rearrange("p (t h) -> p t h", t=NT)
        rstd = view(o + 357, 2)
        mx = view(o + 359, 16).rearrange("p (t h) -> p t h", t=NT)
        ssum = view(o + 375, 16).rearrange("p (t h) -> p t h", t=NT)
        epsc = view(o + 391, 1)
        NEP = NE + 2
        mask = view(o + 392, NT * NEP).rearrange("p (t e) -> p t e", t=NT)
        gate = view(o + 460, NT * NEP).rearrange("p (t e) -> p t e", t=NT)
        slot1 = view(o + 528, NT * NEP).rearrange("p (t e) -> p t e", t=NT)
        rl = view(o + 596, NT * NE).rearrange("p (t e) -> p t e", t=NT)
        br = view(o + 660, NE)
        bgu = view(o + 692, NE * 16).rearrange("p (e f) -> p e f", e=NE)
        selg = view(o + 1204, 512).rearrange("p (q t h c) -> p q t h c", q=2, t=NT, h=2)
        need = view(o + 1716, 1)[0:MORE, :]
        pass_c = view(o + 1717, 2)[0:MORE, :]
        above, expert_no = pass_c[:, 0:1], pass_c[:, 1:2]
        place = view(o + 1719, LIST)[0:MORE, :]
        iota_c = view(o + 1735, WIDE)
        wide_f = view(o + 1863, NE)[0:1, :]
        stats4 = view(o + 1895, 48).rearrange("p (t a b) -> p t a b", t=NT, a=4)
        assert o + 1943 <= 27400
        relb_sb = sb("relb_sb", [NB, H])
        oneh_sb = sb("oneh_sb", [NB, S + P])
        tab_sb = sb("tab_sb", [H, S + P])
        wr_sb = sb("wr_sb", [P, KD, NE])
        idxu = sb("idxu", [P, NT, 8], U32)
        more = sb("more", [1, LIST + 1], I32)
        wide = sb("wide", [1, NE], I32)
        pT_sb = view(10496, 512).rearrange("p (k t) -> p k t", k=2)
        wpp_sb = view(20856, 2048).rearrange("p (k d) -> p k d", k=2)
        vb = view(13688, 512)

        e_in = [sem(f"expert_slot{i}_in") for i in range(ES)]
        arrived = [sem(f"slot{i}_arrived") for i in range(NS)]
        chunk_used = sem("chunk_used")
        small_in, late_in = sem("small_in"), sem("late_in")
        xT_in, x_in = [sem("xT_in0"), sem("xT_in1")], sem("x_in")
        first_in = [sem("first_in0"), sem("first_in1")]
        relb_in = sem("relb_in")
        tab_out, hankel_in, ln_in = sem("tab_out"), sem("hankel_in"), sem("ln_in")
        consts = sem("consts")
        pool_chain = sem("pool_chain")
        v_chain = sem("v_chain")
        tile_done, tile_out = sem("tile_done"), sem("tile_out")
        wi_done, wi_out = sem("wi_done"), sem("wi_out")
        dots_done, relu_out, relu_used = sem("dots_done"), sem("relu_out"), sem("relu_used")
        score_masked = sem("score_masked")
        chosen, amask_ready = sem("chosen"), sem("amask_ready")
        v_done, v_out = sem("v_done"), sem("v_out")
        tab_done, tab_ready = sem("tab_done"), sem("tab_ready")
        lg_done, lg_out = sem("lg_done"), sem("lg_out")
        max_ready, exp_ready, probs_ready = sem("max_ready"), sem("exp_ready"), sem("probs_ready")
        pt_done, pt_out, pv_done, attn_out = sem("pt_done"), sem("pt_out"), sem("pv_done"), sem("attn_out")
        bq_ready = sem("bq_ready")
        ple_in, pple_done, pple_out = sem("ple_in"), sem("pple_done"), sem("pple_out")
        conv_y, mean_done, sq_ready, var_done = sem("conv_y"), sem("mean_done"), sem("sq_ready"), sem("var_done")
        centred = sem("centred")
        std_ready, norm_ready, csig_ready, conv_ready = (
            sem("std_ready"), sem("norm_ready"), sem("csig_ready"), sem("conv_ready"))
        y_done, y_out, merged_ready = sem("y_done"), sem("y_out"), sem("merged_ready")
        mix_done = sem("mix_done")
        var1, std1, x1_ready = sem("var1"), sem("std1"), sem("x1_ready")
        xt_done, x1T_out = sem("x1T_done"), sem("x1T_out")
        rl_done, rl_shift, rl_exp = sem("rl_done"), sem("rl_shift"), sem("rl_exp")
        mask_ready, cum_done, more_ready = sem("mask_ready"), sem("cum_done"), sem("more_ready")
        rank_done, list_done = sem("rank_done"), sem("list_done")

        slot_moved = sem("slot_moved")
        wide_ready = sem("wide_ready")
        selw_ready, gathw_done, xtw_ready = sem("selw_ready"), sem("gathw_done"), sem("xtw_ready")
        selw_onehot = sem("selw_onehot")
        selg_ready, selg_part, sel_ready = sem("selg_ready"), sem("selg_part"), sem("sel_ready")
        gath_done, xt_half, xt_ready = sem("gath_done"), sem("xt_half"), sem("xt_ready")
        gT_done, acc_out = sem("gT_done"), sem("acc_out")
        first_zero, first_rows = sem("first_zero"), sem("first_rows")
        sgt_done, g2_out, gu_done, h_out = sem("sgt_done"), sem("g2_out"), sem("gu_done"), sem("h_out")
        comb_done, t_done, t_read = sem("comb_done"), sem("t_done"), sem("t_read")
        sw_biased, sw_summed, sw_prod = sem("sw_biased"), sem("sw_summed"), sem("sw_prod")
        sig_in, sig_out, act_ready = sem("sig_in"), sem("sig_out"), sem("act_ready")
        d_half, d_done = sem("d_half"), sem("d_done")
        y_half, y_sb_out = sem("y_half"), sem("y_sb_out")
        hT_done, hT_out, pg_done, pge_ready = sem("hT_done"), sem("hT_out"), sem("pg_done"), sem("pge_ready")
        var2, std2, t_chain, out_ready, out_done = (
            sem("var2"), sem("std2"), sem("t_chain"), sem("out_ready"), sem("out_done"))

        def wslot(i):
            return ring[:, i % NS, :]

        def w_view(i):
            what, _, n = FRONT[i]
            kt = 4 if what in ("oa", "oc") else KD
            return wslot(i)[:, 0:kt * n].rearrange("p (k c) -> p k c", k=kt)

        src = {"in": w_in, "oa": w_oa, "oc": w_oc, "out": w_out}

        def wait_chunk(eng, i):
            eng.wait_ge(arrived[i % NS], 16 * (i // NS + (i % NS > 0)))

        def front_used(i):
            what, c0, n = FRONT[i]
            if c0 == KI0:
                return wi_done, 2
            if c0 in (V0, V0 + 256) and what == "in":
                return v_done, 2 + 2 * (c0 > V0)
            if what == "in":
                return tile_done, 2 * sum(w == "in" and b != KI0 and not V0 <= b < QI0 for w, b, _ in FRONT[:i + 1])
            if what == "out":
                return mix_done, 2 + c0 // 256
            return y_done, 4 * (i - FRONT.index(("oa", 0, 512)) + 1)

        def expert_used(e, c):
            if c == KD - 1:
                return gu_done, e * 4 + 4
            if c == CPE - 1:
                return d_done, e + 1
            return chunk_used, e * (CPE - 2) + (c + 1 if c < KD else c)

        def expert_w(q, c):
            i = (q * CPE + c) % ES
            return ring[:, (NF + i) % NS, :] if i < NS else extra[i - NS]

        def expert_source(e, c):
            if c < KD:
                return w_gu[bass.ds(e, 1), c * P:(c + 1) * P, :].rearrange("e p d -> p (e d)")
            f = 2 * (c - KD)
            return w_dn[bass.ds(e, 1), f * P:(f + 2) * P, :].rearrange("e (k p) d -> p (e k) d", p=P)

        def load_expert(sp, e, q, c):
            w = expert_w(q, c)
            if c >= KD:
                w = w.rearrange("p (k d) -> p k d", k=2)
            sp.dma_start(w, expert_source(e, c)).then_inc(e_in[(q * CPE + c) % ES], 16)

        def expert_in(step, q, c):
            n = q * CPE + c
            return e_in[n % ES], step * (16 * UNROLL * CPE // ES) + 16 * (n // ES + 1)

        def gather(pe):
            for k in range(KD):
                for t in range(NT):
                    mm = pe.matmul(bank[4 + k // 4][:, (k % 4) * P:(k % 4 + 1) * P], x1[:, t, k * P:(k + 1) * P],
                                   sel[:, t, :, :], start=(t == 0), stop=(t == NT - 1))
            return mm

        def gate_up(pe, chunk, q):
            def product(k, n, w):
                a = (k % 2) * CAP
                return pe.matmul(bank[n][a:a + CAP, :], XT[:, k, q, :], w[:, n * 512:(n + 1) * 512],
                                 start=(k < 2), stop=(k >= KD - 2))

            for k in range(0, KD - 2, 2):
                ws = chunk(k), chunk(k + 1)
                for n in BANK_ORDER:
                    for half in range(2):
                        mm = product(k + half, n, ws[half])
                        if n == BANK_ORDER[-1]:
                            mm.then_inc(chunk_used, 1)
            for k in range(KD - 2, KD):
                w = chunk(k)
                for n in BANK_ORDER:
                    mm = product(k, n, w)
                    if k == KD - 1:
                        mm.then_inc(gu_done, 1)
                    elif n == BANK_ORDER[-1]:
                        mm.then_inc(chunk_used, 1)

        def gather_wide(pe):
            for k in range(KD):
                for t in range(NT):
                    mm = pe.matmul(bank[4 + k // 4][:, (k % 4) * P:(k % 4 + 1) * P], x1[:, t, k * P:(k + 1) * P],
                                   sel_w[:, t, :], start=(t == 0), stop=(t == NT - 1))
            return mm

        def gate_up_wide(pe, chunk):
            for k in range(KD):
                w = chunk(k)
                for n in BANK_ORDER:
                    mm = pe.matmul(bank[n][:, :], XT_w[:, k, :], w[:, n * 512:(n + 1) * 512],
                                   start=(k == 0), stop=(k == KD - 1))
                    if k == KD - 1:
                        mm.then_inc(gu_done, 1)
                    elif n == BANK_ORDER[-1]:
                        mm.then_inc(chunk_used, 1)

        def turn(pe, hh):
            for g in range(2):
                for f in range(4):
                    at = g * 1024 + (4 * hh + f) * P
                    mm = pe.transpose(bank[4 + 2 * hh + g][:, f * P:(f + 1) * P], hsb[:, at:at + P], ident)
            return mm

        def down(pe, w, f):
            for n in range(2):
                for half in range(2):
                    a = half * CAP
                    mm = pe.matmul(bank[6 + n][a:a + CAP, :], act_sb[:, f + half, :],
                                   w[:, half * 1024 + n * 512:half * 1024 + (n + 1) * 512], start=(f == 0), stop=(f == 6))
                if f == 6:
                    mm.then_inc(d_half if n == 0 else d_done, 1)
            if f < 6:
                mm.then_inc(chunk_used, 1)

        def down_wide(pe, w, f):
            for n in range(2):
                for kk in range(2):
                    mm = pe.matmul(bank[6 + n][:, :], act_w[:, f + kk, :],
                                   w[:, kk * 1024 + n * 512:kk * 1024 + (n + 1) * 512],
                                   start=(f + kk == 0), stop=(f + kk == 7))
                if f == 6:
                    mm.then_inc(d_half if n == 0 else d_done, 1)
            if f < 6:
                mm.then_inc(chunk_used, 1)

        def combine(pe, q, j):
            return pe.matmul(bank[j][:, :], G2[:, q, (j // 2) * P:(j // 2 + 1) * P],
                             ysb[:, (j % 2) * 512:(j % 2) * 512 + 512], start=True, stop=True)

        def acc_part(j):
            return acc[:, j // 2, (j % 2) * 512:(j % 2) * 512 + 512]

        def halves(b):
            return bank[b][:, :].rearrange("p (f h c) -> p f h c", f=4, h=2)


        def swiglu(v, e, hh, n):
            fs = slice(4 * hh, 4 * hh + 4)
            for g, dst in enumerate((gt, up)):
                v.wait_ge(t_done, n)
                src_ = halves(4 + 2 * hh + g)
                nc.vector.tensor_tensor(dst[:, fs, :], src_[:, :, 0, :],
                                        bgu_of(e, g, hh).to_broadcast([P, 4, CAP]), ALU.add).then_inc(sw_biased, 1)
                v.wait_ge(sw_biased, n * 2 - 1 + g)
                nc.vector.tensor_tensor(dst[:, fs, :], src_[:, :, 1, :], dst[:, fs, :], ALU.add
                                        ).then_inc(sw_summed, 1)
            v.wait_ge(sw_summed, n * 2 - 1)
            nc.vector.tensor_scalar(gt[:, fs, :], gt[:, fs, :], LIMIT, None, ALU.min).then_inc(sig_in, 1)
            v.wait_ge(sw_summed, n * 2)
            nc.vector.tensor_scalar(up[:, fs, :], up[:, fs, :], LIMIT, -LIMIT, ALU.min, ALU.max).then_inc(t_read, 1)
            v.wait_ge(t_read, n)
            v.wait_ge(sig_in, n)
            nc.vector.scalar_tensor_tensor(up[:, fs, :], up[:, fs, :], 1.0, gt[:, fs, :], ALU.add, ALU.mult
                                           ).then_inc(sw_prod, 1)
            v.wait_ge(sw_prod, n)
            v.wait_ge(sig_out, n)
            nc.vector.tensor_tensor(act_sb[:, fs, :], up[:, fs, :], sg[:, fs, :], ALU.mult).then_inc(act_ready, 1)

        def swiglu_wide(v, e, hh, n):
            if hh == 1:
                v.wait_ge(act_ready, n - 1)
            for g, dst in enumerate((gt_w, up_w)):
                v.wait_ge(t_done, n)
                nc.vector.tensor_tensor(dst, bank[4 + 2 * hh + g][:, :].rearrange("p (f c) -> p f c", f=4),
                                        bgu_of(e, g, hh).to_broadcast([P, 4, WIDE]), ALU.add).then_inc(sw_biased, 1)
            v.wait_ge(sw_biased, n * 2)
            nc.vector.sem_inc(sw_summed, 2)
            nc.vector.tensor_scalar(gt_w, gt_w, LIMIT, None, ALU.min).then_inc(sig_in, 1)
            nc.vector.tensor_scalar(up_w, up_w, LIMIT, -LIMIT, ALU.min, ALU.max).then_inc(t_read, 1)
            v.wait_ge(t_read, n)
            v.wait_ge(sig_in, n)
            nc.vector.scalar_tensor_tensor(up_w, up_w, 1.0, gt_w, ALU.add, ALU.mult).then_inc(sw_prod, 1)
            v.wait_ge(sw_prod, n)
            v.wait_ge(sig_out, n)
            nc.vector.tensor_tensor(act_w[:, 4 * hh:4 * hh + 4, :], up_w, sg_w, ALU.mult).then_inc(act_ready, 1)

        def bgu_of(e, g, hh):
            at = g * 8 + 4 * hh
            return bgu[:, bass.ds(e, 1), at:at + 4].rearrange("p e f -> p (e f)").unsqueeze(2)

        def select_wide(v, e, q):
            nc.vector.tensor_tensor(sel_w, iota_c.unsqueeze(1).to_broadcast([P, NT, WIDE]),
                                    slot1[:, :, bass.ds(e, 1)].to_broadcast([P, NT, WIDE]),
                                    ALU.is_equal).then_inc(selw_onehot, 1)
            v.wait_ge(selw_onehot, e + 1)
            nc.vector.tensor_scalar(slot1[:, :, bass.ds(e, 1)], slot1[:, :, bass.ds(e, 1)], float(CAP),
                                    None, ALU.subtract).then_inc(slot_moved, 1)
            for t in range(NT):
                nc.vector.tensor_scalar(selg[:, q, t, :, :].rearrange("p h c -> p (h c)"), sel_w[:, t, :],
                                        gate[:, t, bass.ds(e, 1)], None, ALU.mult
                                        ).then_inc(selw_ready if t == NT - 1 else selg_part, 1)

        def one_hot(v, first):
            nc.vector.tensor_tensor(sel[:, :, :, :],
                                    iota_c[:, 0:CAP].unsqueeze(1).unsqueeze(1).to_broadcast([P, NT, 2, CAP]),
                                    slot1[:, :, bass.ds(first, 2)].unsqueeze(3).to_broadcast([P, NT, 2, CAP]),
                                    ALU.is_equal).then_inc(sel_ready, 1)

        def gates_by_slot(v, first, n0):
            v.wait_ge(sel_ready, n0)
            for q in range(2):
                for t in range(NT):
                    nc.vector.tensor_tensor(
                        selg[:, q, t, :, :], sel[:, t, q:q + 1, :].to_broadcast([P, 2, CAP]),
                        gate[:, t, bass.ds(first + q, 1)].unsqueeze(2).to_broadcast([P, 2, CAP]),
                        ALU.mult).then_inc(selg_ready if (q, t) == (1, 1) else selg_part, 1)

        def select(v, first, n0):
            one_hot(v, first)
            gates_by_slot(v, first, n0)

        def xt_out(a, n):
            a.wait_ge(gath_done, n)
            for b in range(2):
                a.activation(XT[:, 4 * b:4 * b + 4, :, :], bank[4 + b][:, :].rearrange("p (k q c) -> p k q c", k=4, q=2),
                             ACT.Identity).then_inc(xt_half if b == 0 else xt_ready, 1)

        with nc.Block() as block:
            @block.sync
            def _(sp):
                HK, (what, c0, n) = KD // 2, FRONT[0]
                for half in range(2):
                    ks = slice(half * HK, (half + 1) * HK)
                    rows = slice(half * HK * P, (half + 1) * HK * P)
                    sp.dma_start(xT_sb[:, ks, :], xT[rows, :].rearrange("(k p) t -> p k t", p=P)).then_inc(xT_in[half], 16)
                    sp.dma_start(w_view(0)[:, ks, :], src[what][rows, c0:c0 + n].rearrange("(k p) c -> p k c", p=P)
                                 ).then_inc(first_in[half], 16)
                for i, (what, c0, n) in enumerate(FRONT):
                    if i == 0:
                        continue
                    if i >= NS:
                        sp.wait_ge(*front_used(i - NS))
                    sp.dma_start(w_view(i), src[what][:, c0:c0 + n].rearrange("(k p) c -> p k c", p=P)
                                 ).then_inc(arrived[i % NS], 16)
                for c in range(KD):
                    sp.wait_ge(*front_used(NF + c - NS))
                    load_expert(sp, 0, 0, c)
                for c, free in enumerate(((y_out, 8), (merged_ready, 8), (pt_done, 8))):
                    sp.wait_ge(*free)
                    load_expert(sp, 1, 1, c)
                for c in range(KD, CPE):
                    sp.wait_ge(*front_used(NF + c - NS))
                    load_expert(sp, 0, 0, c)
                sp.wait_ge(pple_done, 4)
                load_expert(sp, 1, 1, 3)

            @block.gpsimd
            def _(g):
                n = Tally()
                g.memset(ident, 0.0).then_inc(pool_chain, 1)
                g.memset(flip, 0.0).then_inc(pool_chain, 1)
                g.memset(upper, 1.0).then_inc(pool_chain, 1)
                g.memset(u_sb[:, :, 0:CW - 1], 0.0).then_inc(consts, 1)
                g.memset(ones, 1.0).then_inc(consts, 1)
                g.memset(epsc, EPS).then_inc(consts, 1)
                g.memset(mask[:, :, :], 0.0).then_inc(consts, 1)
                g.memset(gate[:, :, :], 0.0).then_inc(consts, 1)
                g.memset(slot1[:, :, :], 0.0).then_inc(consts, 1)
                g.iota(iota_c, [[1, WIDE]], base=1, channel_multiplier=0,
                       allow_small_or_imprecise_dtypes=True).then_inc(consts, 1)
                g.iota(iota_e, [[1, NE]], base=0, channel_multiplier=0,
                       allow_small_or_imprecise_dtypes=True).then_inc(consts, 1)
                g.wait_ge(pool_chain, 3)
                g.affine_select(out=ident, in_=ident, compare_op=ALU.not_equal, fill=1.0, base=0,
                                pattern=[[-1, P]], channel_multiplier=1).then_inc(consts, 1)
                g.affine_select(out=flip, in_=flip, compare_op=ALU.not_equal, fill=1.0, base=-(P - 1),
                                pattern=[[1, P]], channel_multiplier=1).then_inc(consts, 1)
                g.affine_select(out=upper, in_=upper, compare_op=ALU.is_gt, fill=0.0, base=0,
                                pattern=[[1, P]], channel_multiplier=-1).then_inc(consts, 1)
                g.wait_ge(tab_ready, 1)
                g.dma_start(table, tab_sb[:, :]).then_inc(tab_out, 16)
                g.wait_ge(tab_out, 16)
                skew = bass.AP(tensor=table.tensor, offset=0, ap=[[1, P], [S + P, H], [1, S]])
                g.dma_start(hankel, skew).then_inc(hankel_in, 16)
                g.wait_ge(relu_used, 2 * H)
                g.affine_select(out=score[:, 0:P], in_=score[:, 0:P], compare_op=ALU.is_ge, fill=BELOW,
                                base=0, pattern=[[-1, P]], channel_multiplier=1).then_inc(score_masked, 1)
                g.affine_select(out=score[:, P:3 * P], in_=score[:, P:3 * P], compare_op=ALU.is_ge, fill=BELOW,
                                base=P, pattern=[[-1, S]], channel_multiplier=1).then_inc(score_masked, 1)
                g.wait_ge(chosen, 1)
                g.affine_select(out=amask[:, 0:P], in_=amask[:, 0:P], compare_op=ALU.is_ge, fill=NEG,
                                base=0, pattern=[[-1, P]], channel_multiplier=1).then_inc(amask_ready, 1)
                g.affine_select(out=amask[:, P:3 * P], in_=amask[:, P:3 * P], compare_op=ALU.is_ge, fill=NEG,
                                base=P, pattern=[[-1, S]], channel_multiplier=1).then_inc(amask_ready, 1)

            @block.tensor
            def _(pe):
                tiles = Tally()

                def two(i):
                    if i:
                        wait_chunk(pe, i)
                    for j in range(2):
                        n = tiles.n
                        if n >= 4:
                            pe.wait_ge(tile_out, n - 3)
                        w = w_view(i)
                        for k in range(KD):
                            if n == 0 and k % (KD // 2) == 0:
                                pe.wait_ge(xT_in[2 * k // KD], 16)
                                pe.wait_ge(first_in[2 * k // KD], 16)
                            mm = pe.matmul(bank[n % 4][:, 0:S], w[:, k, j * P:(j + 1) * P], xT_sb[:, k, :],
                                           start=(k == 0), stop=(k == KD - 1))
                        mm.then_inc(tile_done, 1)
                        tiles.up()

                two(0)
                two(1)
                pe.wait_ge(relb_in, 32)
                pe.matmul(bank[7][0:H, 0:S + P], relb_sb[:, :], oneh_sb[:, :], start=True, stop=True).then_inc(tab_done, 1)
                wait_chunk(pe, 2)
                w = w_view(2)
                for k in range(KD):
                    for half in range(2):
                        mm = pe.matmul(bank[6][half * 64:half * 64 + 64, 0:S], w[:, k, 0:64], xT_sb[:, k, :],
                                       start=(k == 0), stop=(k == KD - 1))
                mm.then_inc(wi_done, 1)
                pe.wait_ge(tab_ready, 1)
                for t in range(NT):
                    for k in range(KD):
                        mm = pe.matmul(bank[7][:, t * 8:t * 8 + 8], xT_sb[:, k, t * P:(t + 1) * P], w[:, k, 64:72],
                                       start=(k == 0), stop=(k == KD - 1))
                mm.then_inc(wi_done, 1)
                two(3)
                pe.wait_ge(tile_out, 4)
                pe.wait_ge(wi_out, 2)
                for g in range(0, H, 2):
                    if g >= 4:
                        pe.wait_ge(relu_out, g - 2)
                    for h in (g, g + 1):
                        a = (h % 2) * 64
                        pe.matmul(bank[4 + h % 4][:, 0:P], qiT[a:a + 64, h // 2, 0:P], kiT[a:a + 64, 0:P],
                                  start=True, stop=True)
                    for h in (g, g + 1):
                        a = (h % 2) * 64
                        pe.matmul(bank[4 + h % 4][:, P:3 * P], qiT[a:a + 64, h // 2, P:S], kiT[a:a + 64, 0:S],
                                  start=True, stop=True).then_inc(dots_done, 1)
                two(4)
                two(5)
                two(6)
                pe.wait_ge(relu_out, 8)
                for j in range(2):
                    wait_chunk(pe, 7 + j)
                    for t in range(NT):
                        for k in range(KD):
                            mm = pe.matmul(bank[4 + 2 * j + t][:, 0:256], xT_sb[:, k, t * P:(t + 1) * P],
                                           w_view(7 + j)[:, k, :], start=(k == 0), stop=(k == KD - 1))
                        mm.then_inc(v_done, 1)
                two(9)
                pe.wait_ge(tile_out, 12)
                pe.wait_ge(hankel_in, 16)
                for h in range(H):
                    if h < 4:
                        pe.wait_ge(v_out, h + 1)
                    else:
                        pe.wait_ge(lg_out, h - 3)
                    a = (h % 2) * 64
                    b = bank[4 + h % 4]
                    pe.matmul(b[:, 0:P], qT[a:a + 64, h // 2, 0:P], kT[a:a + 64, h // 2, 0:P], start=True, stop=False)
                    pe.matmul(b[:, 0:P], flip, hankel[:, h, P:S], start=False, stop=True)
                    pe.matmul(b[:, P:3 * P], qT[a:a + 64, h // 2, P:S], kT[a:a + 64, h // 2, :], start=True, stop=False)
                    pe.matmul(b[:, P:3 * P], flip, hankel[:, h, :], start=False, stop=True).then_inc(lg_done, 1)
                for i in range(10, 17):
                    two(i)

                def turn_probs(h):
                    if h >= 2:
                        pe.wait_ge(pt_out, h - 1)
                    for j, at in enumerate((0, P, 2 * P)):
                        mm = pe.transpose(bank[4 + h % 2][:, j * P:(j + 1) * P], logit[:, h, at:at + P], ident)
                    mm.then_inc(pt_done, 1)

                def times_values(h):
                    pe.wait_ge(pt_out, h + 1)
                    a = (h % 2) * 64
                    b = bank[6]
                    vg = slice(h * 64, h * 64 + 64)
                    pe.matmul(b[a:a + 64, 0:P], v_sb[:, 0, vg], pT_h[:, h % 2, 0:P], start=True, stop=True)
                    pe.matmul(b[a:a + 64, P:S], v_sb[:, 0, vg], pT_h[:, h % 2, P:S], start=True, stop=False)
                    pe.matmul(b[a:a + 64, P:S], v_sb[:, 1, vg], pT_h[:, h % 2, S:S + P],
                              start=False, stop=True).then_inc(pv_done, 1)

                pe.wait_ge(probs_ready, 2)
                pe.wait_ge(lg_out, 8)
                for g in range(0, H, 2):
                    turn_probs(g)
                    turn_probs(g + 1)
                    two(17 + g // 2)
                    if g:
                        pe.wait_ge(attn_out, g // 2)
                    times_values(g)
                    times_values(g + 1)
                    if g == 4:
                        pe.wait_ge(conv_y, 1)
                        for a in range(4):
                            mm = pe.matmul(bank[7][:, 0:S], ones, cy[:, a, :], start=(a == 0), stop=(a == 3))
                        mm.then_inc(mean_done, 1)
                pe.wait_ge(sq_ready, 1)
                pe.wait_ge(pt_out, 8)
                for a in range(4):
                    mm = pe.matmul(bank[5][:, 0:S], ones, cg[:, a, :], start=(a == 0), stop=(a == 3))
                mm.then_inc(var_done, 1)
                pe.wait_ge(attn_out, 4)
                pe.wait_ge(tile_out, 36)

                def project(i0, rhs, n0):
                    for c in range(8):
                        i = i0 + c // 4
                        if c % 4 == 0:
                            wait_chunk(pe, i)
                        n = n0 + c
                        if n >= 4:
                            pe.wait_ge(y_out, n - 3)
                        for k in range(4):
                            mm = pe.matmul(bank[n % 4][:, 0:S], w_view(i)[:, k, (c % 4) * P:(c % 4 + 1) * P],
                                           rhs[:, k, :], start=(k == 0), stop=(k == 3))
                        mm.then_inc(y_done, 1)
                project(21, attnT, 0)
                pe.wait_ge(conv_ready, 1)
                project(23, cy, 8)
                for t in range(NT):
                    for j in range(4):
                        if t == 0:
                            wait_chunk(pe, 25 + j)
                        for k in range(KD):
                            if t == 0 and j == 0:
                                pe.wait_ge(merged_ready, k + 1)
                            mm = pe.matmul(bank[4 + 2 * t + j // 2][:, (j % 2) * 256:(j % 2) * 256 + 256],
                                           merged[:, k, t * P:(t + 1) * P], w_view(25 + j)[:, k, :],
                                           start=(k == 0), stop=(k == KD - 1))
                        if t == 1 or j == 3:
                            mm.then_inc(mix_done, 1)
                def embed(n):
                    t, j = n // 2, n % 2
                    for k in range(2):
                        mm = pe.matmul(bank[EMBED_BANK[n]][:, :], pT_sb[:, k, t * P:(t + 1) * P],
                                       wpp_sb[:, k, j * 512:(j + 1) * 512], start=(k == 0), stop=(k == 1))
                    mm.then_inc(pple_done, 1)

                def turn_x1(t):
                    for k in range(KD):
                        if k % 4 == 0:
                            pe.wait_ge(x1_ready, 2 * t + k // 4 + 1)
                        mm = pe.transpose(bank[2 * t + k // 4][:, (k % 4) * P:(k % 4 + 1) * P],
                                          x1[:, t, k * P:(k + 1) * P], ident)
                        if k % 4 == 3:
                            mm.then_inc(xt_done, 1)

                def route(t):
                    for k in range(KD):
                        if k % 4 == 0:
                            pe.wait_ge(x1T_out, 2 * t + k // 4 + 1)
                        mm = pe.matmul(bank[ROUTE_BANK[t]][:, 0:NE], x1T[:, k, t * P:(t + 1) * P],
                                       wr_sb[:, k, :], start=(k == 0), stop=(k == KD - 1))
                    mm.then_inc(rl_done, 1)

                turn_x1(0)
                pe.wait_ge(ple_in, 32)
                pe.wait_ge(var1, 1)
                embed(0)
                route(0)
                turn_x1(1)
                pe.wait_ge(var1, 2)
                embed(1)
                route(1)
                embed(2)
                pe.wait_ge(mask_ready, 2)
                pe.wait_ge(pple_out, 2)
                pe.matmul(bank[6][:, 0:NE], upper, mask[:, 0, 0:NE], start=True, stop=True)
                pe.matmul(bank[6][:, NE:2 * NE], upper, mask[:, 1, 0:NE], start=True, stop=False)
                pe.matmul(bank[6][:, NE:2 * NE], ones, mask[:, 0, 0:NE], start=False, stop=True)
                for t in range(NT):
                    pe.matmul(bank[6][0:1, 2 * NE:3 * NE], ones[:, 0:1], mask[:, t, 0:NE], start=(t == 0), stop=(t == NT - 1))
                for j in range(NMORE):
                    for t in range(NT):
                        mm = pe.matmul(bank[7][j * NE:(j + 1) * NE, 0:1], mask[:, t, 0:NE], ones[:, 0:1],
                                       start=(t == 0), stop=(t == NT - 1))
                mm.then_inc(cum_done, 1)
                embed(3)
                pe.wait_ge(more_ready, 1)
                pe.matmul(bank[7][0:MORE, 1:2], upper[0:MORE, 0:MORE], need, start=True, stop=True).then_inc(rank_done, 1)
                pe.wait_ge(sel_ready, 1)
                gather(pe).then_inc(gath_done, 1)
                pe.wait_ge(more_ready, 2)
                pe.matmul(bank[6][0:1, 3 * NE:3 * NE + LIST], expert_no, place, start=True, stop=True)
                pe.matmul(bank[6][0:1, 3 * NE + LIST:3 * NE + LIST + 1], need, ones[0:MORE, 0:1], start=True, stop=True
                          ).then_inc(list_done, 1)

            @block.scalar
            def _(a):
                a.dma_start(relb_sb[:, :], relb).then_inc(relb_in, 16)
                a.dma_start(oneh_sb[:, :], onehot).then_inc(relb_in, 16)
                a.dma_start(bT_sb, bT).then_inc(small_in, 16)
                a.dma_start(bki_sb, bki).then_inc(small_in, 16)
                a.dma_start(bwi, b_in[WI0:WI0 + 8].partition_broadcast(P)).then_inc(small_in, 16)
                a.dma_start(pass_c, passes).then_inc(small_in, 16)
                a.dma_start(vb, b_in[V0:V0 + 512].partition_broadcast(P)).then_inc(late_in, 16)
                a.dma_start(dw, dwT.rearrange("p (a j) -> p a j", a=4)).then_inc(late_in, 16)
                a.dma_start(cv, convT.rearrange("p (j a) -> p j a", j=3)).then_inc(late_in, 16)
                a.dma_start(wr_sb[:, :, :], w_r.rearrange("(k p) e -> p k e", p=P)).then_inc(late_in, 16)
                a.dma_start(br, b_r.partition_broadcast(P)).then_inc(late_in, 16)
                a.dma_start(bgu, bguT.rearrange("p (e f) -> p e f", e=NE)).then_inc(late_in, 16)
                a.dma_start(x_sb, x.rearrange("(t p) d -> p t d", p=P)).then_inc(x_in, 16)
                a.wait_ge(small_in, 16 * 4)

                cnt = Tally()

                def evac(dst, func, bias, scale=1.0):
                    n = cnt.n
                    a.wait_ge(tile_done, n + 1)
                    a.activation(dst, bank[n % 4][:, 0:S], func, bias=bias, scale=scale).then_inc(tile_out, 1)
                    cnt.up()

                for j in range(4):
                    evac(qiT[:, j, :], ACT.Identity, bT_sb[:, j:j + 1])
                a.wait_ge(tab_done, 1)
                a.activation(tab_sb[:, :], bank[7][0:H, 0:S + P], ACT.Identity).then_inc(tab_ready, 1)
                a.wait_ge(wi_done, 1)
                a.activation(kiT, bank[6][:, 0:S], ACT.Identity, bias=bki_sb).then_inc(wi_out, 1)
                a.wait_ge(bq_ready, 1)
                for j in range(2):
                    evac(qT[:, j, :], ACT.Identity, bq[:, j:j + 1], 0.125)
                for h in range(H):
                    a.wait_ge(dots_done, h + 1)
                    if h >= 2:
                        a.wait_ge(relu_used, 2 * h - 2)
                    a.activation(relu[:, h % 2, :], bank[4 + h % 4][:, 0:3 * P], ACT.Relu).then_inc(relu_out, 1)
                for j in range(2, 4):
                    evac(qT[:, j, :], ACT.Identity, bq[:, j:j + 1], 0.125)
                for j in range(4):
                    evac(kT[:, j, :], ACT.Identity, bT_sb[:, 8 + j:9 + j])

                def conv_pair(c):
                    for j in range(2):
                        evac(cy[:, 2 * c + j, :], ACT.Identity, bT_sb[:, 12 + 2 * c + j:13 + 2 * c + j])
                    for j in range(2):
                        evac(cg[:, 2 * c + j, :], ACT.Sigmoid, bT_sb[:, 16 + 2 * c + j:17 + 2 * c + j])

                conv_pair(0)
                a.wait_ge(max_ready, 2)
                for h in range(H):
                    for t, (lo, n) in enumerate(((0, P), (P, S))):
                        a.activation(logit[:, h, lo:lo + n], logit[:, h, lo:lo + n], ACT.Exp,
                                     bias=mx[:, t, h:h + 1], accum_out=ssum[:, t, h:h + 1]).then_inc(exp_ready, 1)
                conv_pair(1)
                for j in range(8):
                    evac(sga[:, j, :], ACT.Sigmoid, bT_sb[:, 20 + j:21 + j])
                a.wait_ge(lg_done, 8)
                a.dma_start(wpp_sb, w_pp.rearrange("(k p) d -> p k d", p=P)).then_inc(ple_in, 16)
                for g in range(0, H, 2):
                    for h in (g, g + 1):
                        a.wait_ge(pt_done, h + 1)
                        if h >= 2:
                            a.wait_ge(pv_done, h - 1)
                        a.activation(pT_h[:, h % 2, :], bank[4 + h % 2][:, 0:3 * P], ACT.Identity).then_inc(pt_out, 1)
                    for j in (g, g + 1):
                        evac(sgc[:, j, :], ACT.Sigmoid, bT_sb[:, 28 + j:29 + j])
                    if g == 6:
                        a.wait_ge(centred, 1)
                        a.activation(cg, cy, ACT.Square).then_inc(sq_ready, 1)
                    a.wait_ge(pv_done, g + 2)
                    a.activation(attnT[:, g // 2, :], bank[6][:, 0:S], ACT.Identity).then_inc(attn_out, 1)
                a.wait_ge(conv_y, 1)
                a.dma_start(pT_sb, pT.rearrange("(k p) t -> p k t", p=P)).then_inc(ple_in, 16)
                a.wait_ge(var_done, 1)
                a.activation(std, bank[5][:, 0:S], ACT.Sqrt, bias=epsc, scale=1.0 / CC).then_inc(std_ready, 1)
                a.dma_start(lng1, ln1g.partition_broadcast(P)).then_inc(ln_in, 16)
                a.wait_ge(norm_ready, 4)
                a.activation(cg, cy, ACT.Sigmoid).then_inc(csig_ready, 1)
                a.wait_ge(conv_ready, 1)
                a.dma_start(lnb1, ln1b.partition_broadcast(P)).then_inc(ln_in, 16)

                def root(t):
                    a.wait_ge(var1, t + 1)
                    a.activation(rstd[:, t:t + 1], mv[:, t, 1:2], ACT.Sqrt, bias=epsc).then_inc(std1, 1)

                def embedded(n):
                    a.wait_ge(pple_done, n + 1)
                    a.activation(pple[:, n // 2, (n % 2) * 512:(n % 2) * 512 + 512], bank[EMBED_BANK[n]][:, :],
                                 ACT.Identity
                                 ).then_inc(pple_out, 1)

                def turned(t):
                    for b in range(2):
                        a.wait_ge(xt_done, 2 * t + b + 1)
                        a.activation(x1T[:, 4 * b:4 * b + 4, t * P:(t + 1) * P],
                                     bank[2 * t + b][:, :].rearrange("p (k t) -> p k t", k=4), ACT.Identity
                                     ).then_inc(x1T_out, 1)

                root(0)
                turned(0)
                embedded(0)
                root(1)
                turned(1)
                embedded(1)
                embedded(2)
                a.wait_ge(rl_shift, 2)
                a.activation(rl[:, :, :], rl[:, :, :], ACT.Exp).then_inc(rl_exp, 1)
                embedded(3)
                xt_out(a, 1)

            @block.vector
            def _(v):
                c = Tally()
                v.wait_ge(small_in, 16 * 4)
                nc.vector.tensor_scalar(bq, bT_sb[:, 4:8], 0.125, None, ALU.mult).then_inc(bq_ready, 1)
                v.wait_ge(wi_done, 2)
                nc.vector.tensor_tensor(wsc, bank[7][:, 0:16].rearrange("p (t h) -> p t h", t=NT),
                                        bwi.unsqueeze(1).to_broadcast([P, NT, 8]), ALU.add).then_inc(v_chain, 1)
                v.wait_ge(v_chain, c.up())
                nc.vector.tensor_scalar(wsc, wsc, IDX_SCALE, None, ALU.mult).then_inc(wi_out, 1)
                v.wait_ge(wi_out, 2)
                for h in range(H):
                    v.wait_ge(relu_out, h + 1)
                    for t, (lo, n) in enumerate(((0, P), (P, S))):
                        if h == 0:
                            i = nc.vector.tensor_scalar(score[:, lo:lo + n], relu[:, 0, lo:lo + n],
                                                        wsc[:, t, 0:1], None, ALU.mult)
                        else:
                            v.wait_ge(relu_used, 2 * h - 1 + t)
                            i = nc.vector.scalar_tensor_tensor(score[:, lo:lo + n], relu[:, h % 2, lo:lo + n],
                                                               wsc[:, t, h:h + 1], score[:, lo:lo + n],
                                                               ALU.mult, ALU.add)
                        i.then_inc(relu_used, 1)
                v.wait_ge(score_masked, 2)
                for r in range(TOPK // 8):
                    for t, (lo, n) in enumerate(((0, P), (P, S))):
                        if r:
                            v.wait_ge(v_chain, c.n - 1)
                        now = rest if r else score
                        nc.vector.max(top8[:, t, :], now[:, lo:lo + n]).then_inc(v_chain, 1)
                        v.wait_ge(v_chain, c.up())
                        nc.vector.match_replace(rest[:, lo:lo + n], top8[:, t, :], now[:, lo:lo + n],
                                                TAKEN).then_inc(v_chain, 1)
                        c.up()
                v.wait_ge(v_chain, c.n)
                nc.vector.tensor_scalar(amask, rest, -3.2e38, NEG, ALU.is_gt, ALU.mult).then_inc(chosen, 1)
                v.wait_ge(late_in, 16 * 6)
                for n in range(4):
                    j, t = n // 2, n % 2
                    v.wait_ge(v_done, n + 1)
                    nc.vector.tensor_tensor(v_sb[:, t, j * 256:(j + 1) * 256], bank[4 + 2 * j + t][:, 0:256],
                                            vb[:, j * 256:(j + 1) * 256], ALU.add).then_inc(v_out, 1)
                v.wait_ge(amask_ready, 2)
                for h in range(H):
                    v.wait_ge(lg_done, h + 1)
                    nc.vector.tensor_tensor(logit[:, h, :], bank[4 + h % 4][:, 0:3 * P], amask, ALU.add
                                            ).then_inc(lg_out, 1)
                v.wait_ge(lg_out, 8)
                for t, (lo, n) in enumerate(((0, P), (P, S))):
                    nc.vector.tensor_reduce(mx[:, t, :], logit[:, :, lo:lo + n], AX.X, ALU.max).then_inc(v_chain, 1)
                    v.wait_ge(v_chain, c.up())
                    nc.vector.tensor_scalar(mx[:, t, :], mx[:, t, :], -1.0, None, ALU.mult).then_inc(max_ready, 1)
                v.wait_ge(consts, 11)
                for half in range(2):
                    at = slice(2 * half, 2 * half + 2)
                    v.wait_ge(tile_out, 16 + 4 * half)
                    nc.vector.tensor_tensor(u_sb[:, at, CW - 1:U], cy[:, at, :], cg[:, at, :], ALU.mult).then_inc(v_chain, 1)
                    v.wait_ge(v_chain, c.up())
                    for a in (2 * half, 2 * half + 1):
                        nc.vector.tensor_scalar(cy[:, a, :], u_sb[:, a, 0:S], dw[:, a, 0:1], cv[:, 0, a:a + 1],
                                                ALU.mult, ALU.add).then_inc(v_chain, 1)
                    c.up(2)
                    base = c.n
                    with v.Fori(0, (CW - 1) // TAPS) as i:
                        for k in range(TAPS):
                            j = i * TAPS + (k + 1)
                            for a in (2 * half, 2 * half + 1):
                                v.wait_ge(v_chain, i * (2 * TAPS) + (base - 1 + a % 2 + 2 * k))
                                nc.vector.scalar_tensor_tensor(cy[:, a, :], u_sb[:, a, bass.ds(j, S)],
                                                               dw[:, a, bass.ds(j, 1)], cy[:, a, :],
                                                               ALU.mult, ALU.add).then_inc(v_chain, 1)
                    v.wait_ge(v_chain, c.up(2 * (CW - 1)))
                    if half == 0:
                        v.wait_ge(exp_ready, 16)
                        nc.vector.reciprocal(ssum[:, :, :], ssum[:, :, :]).then_inc(v_chain, 1)
                        v.wait_ge(v_chain, c.up())
                        for t, (lo, n) in enumerate(((0, P), (P, S))):
                            nc.vector.tensor_tensor(logit[:, :, lo:lo + n], logit[:, :, lo:lo + n],
                                                    ssum[:, t, :].unsqueeze(2).to_broadcast([P, H, n]), ALU.mult
                                                    ).then_inc(probs_ready, 1)
                nc.vector.sem_inc(conv_y, 1)
                v.wait_ge(mean_done, 1)
                nc.vector.tensor_scalar(mean, bank[7][:, 0:S], 1.0 / CC, None, ALU.mult).then_inc(v_chain, 1)
                v.wait_ge(v_chain, c.up())
                nc.vector.tensor_tensor(cy[:, :, :], cy[:, :, :], mean.unsqueeze(1).to_broadcast([P, 4, S]),
                                        ALU.subtract).then_inc(centred, 1)

                def merge(n):
                    v.wait_ge(y_done, n + 1)
                    b = bank[n % 4][:, 0:S]
                    if n < 8:
                        nc.vector.tensor_tensor(merged[:, n, :], b, sga[:, n, :], ALU.mult).then_inc(y_out, 1)
                    else:
                        m = n - 8
                        nc.vector.tensor_tensor(sgc[:, m, :], b, sgc[:, m, :], ALU.mult).then_inc(y_out, 1)
                        v.wait_ge(y_out, n + 1)
                        nc.vector.tensor_tensor(merged[:, m, :], merged[:, m, :], sgc[:, m, :], ALU.add
                                                ).then_inc(merged_ready, 1)
                v.wait_ge(std_ready, 1)
                nc.vector.reciprocal(std, std).then_inc(v_chain, 1)
                v.wait_ge(v_chain, c.up())
                nc.vector.tensor_tensor(cy[:, :, :], cy[:, :, :], std.unsqueeze(1).to_broadcast([P, 4, S]),
                                        ALU.mult).then_inc(v_chain, 1)
                v.wait_ge(v_chain, c.up())
                for a in range(4):
                    nc.vector.tensor_scalar(cy[:, a, :], cy[:, a, :], cv[:, 1, a:a + 1], cv[:, 2, a:a + 1],
                                            ALU.mult, ALU.add).then_inc(norm_ready, 1)
                for n in range(8):
                    merge(n)
                    if n == 3:
                        v.wait_ge(csig_ready, 1)
                        v.wait_ge(norm_ready, 4)
                        nc.vector.tensor_tensor(cy[:, :, :], cy[:, :, :], cg[:, :, :], ALU.mult).then_inc(conv_ready, 1)
                for n in range(8, 16):
                    merge(n)
                v.wait_ge(x_in, 16)
                for t in range(NT):
                    for j in range(2):
                        v.wait_ge(mix_done, (1, 1, 3, 5)[2 * t + j])
                        nc.vector.scalar_tensor_tensor(res[:, t, j * 512:(j + 1) * 512], x_sb[:, t, j * 512:(j + 1) * 512],
                                                       ALPHA, bank[4 + 2 * t + j][:, :], ALU.mult, ALU.add
                                                       ).then_inc(v_chain, 1)
                        v.wait_ge(v_chain, c.up())
                        nc.vector.bn_stats(stats[:, t, j, :], res[:, t, j * 512:(j + 1) * 512]).then_inc(v_chain, 1)
                        c.up()
                    v.wait_ge(v_chain, c.n)
                    nc.vector.bn_aggr(mv[:, t, :], stats[:, t, :, :]).then_inc(var1, 1)
                    v.wait_ge(var1, t + 1)
                    v.wait_ge(ln_in, 32)
                    nc.vector.scalar_tensor_tensor(res[:, t, 0:512], res[:, t, 0:512], mv[:, t, 0:1], lng1[:, 0:512],
                                                   ALU.subtract, ALU.mult).then_inc(v_chain, 1)
                    v.wait_ge(std1, t + 1)
                    nc.vector.reciprocal(rstd[:, t:t + 1], rstd[:, t:t + 1]).then_inc(v_chain, 1)
                    v.wait_ge(v_chain, c.up(2))
                    nc.vector.scalar_tensor_tensor(x1[:, t, 0:512], res[:, t, 0:512], rstd[:, t:t + 1], lnb1[:, 0:512],
                                                   ALU.mult, ALU.add).then_inc(x1_ready, 1)
                    nc.vector.scalar_tensor_tensor(res[:, t, 512:D], res[:, t, 512:D], mv[:, t, 0:1], lng1[:, 512:D],
                                                   ALU.subtract, ALU.mult).then_inc(v_chain, 1)
                    v.wait_ge(v_chain, c.up())
                    nc.vector.scalar_tensor_tensor(x1[:, t, 512:D], res[:, t, 512:D], rstd[:, t:t + 1], lnb1[:, 512:D],
                                                   ALU.mult, ALU.add).then_inc(x1_ready, 1)
                for t in range(NT):
                    v.wait_ge(rl_done, t + 1)
                    nc.vector.tensor_tensor(rl[:, t, :], bank[ROUTE_BANK[t]][:, 0:NE], br, ALU.add).then_inc(v_chain, 1)
                    v.wait_ge(v_chain, c.up())
                    nc.vector.max(top8[:, t, :], rl[:, t, :]).then_inc(v_chain, 1)
                    v.wait_ge(v_chain, c.up())
                    nc.vector.max_index(idxu[:, t, :], top8[:, t, :], rl[:, t, :]).then_inc(v_chain, 1)
                    v.wait_ge(v_chain, c.up())
                    nc.vector.tensor_copy(idx8[:, t, :], idxu[:, t, :]).then_inc(v_chain, 1)
                    v.wait_ge(v_chain, c.up())
                    for r in range(TOPE):
                        nc.vector.scalar_tensor_tensor(mask[:, t, 0:NE], iota_e, idx8[:, t, r:r + 1],
                                                       mask[:, t, 0:NE], ALU.is_equal, ALU.add
                                                       ).then_inc(mask_ready if r == TOPE - 1 else v_chain, 1)
                        if r < TOPE - 1:
                            v.wait_ge(v_chain, c.up())
                    nc.vector.tensor_scalar(rl[:, t, :], rl[:, t, :], top8[:, t, 0:1], None, ALU.subtract
                                            ).then_inc(rl_shift, 1)
                v.wait_ge(cum_done, 1)
                v.wait_ge(mask_ready, 2)
                nc.vector.tensor_tensor(need, bank[7][0:MORE, 0:1], above, ALU.is_gt).then_inc(more_ready, 1)
                for t in range(NT):
                    nc.vector.scalar_tensor_tensor(slot1[:, t, 0:NE], bank[6][:, t * NE:(t + 1) * NE], 1.0,
                                                   mask[:, t, 0:NE], ALU.add, ALU.mult).then_inc(v_chain, 1)
                v.wait_ge(v_chain, c.up(2))
                one_hot(v, 0)
                v.wait_ge(rl_exp, 1)
                nc.vector.tensor_tensor(gate[:, :, 0:NE], rl[:, :, :], mask[:, :, 0:NE], ALU.mult).then_inc(v_chain, 1)
                v.wait_ge(v_chain, c.up())
                nc.vector.tensor_reduce(rstd[:, 0:2], gate[:, :, 0:NE], AX.X, ALU.add).then_inc(v_chain, 1)
                v.wait_ge(v_chain, c.up())
                nc.vector.reciprocal(rstd[:, 0:2], rstd[:, 0:2]).then_inc(v_chain, 1)
                v.wait_ge(v_chain, c.up())
                nc.vector.tensor_tensor(gate[:, :, 0:NE], gate[:, :, 0:NE],
                                        rstd[:, 0:2].unsqueeze(2).to_broadcast([P, NT, NE]), ALU.mult
                                        ).then_inc(v_chain, 1)
                v.wait_ge(v_chain, c.up())
                gates_by_slot(v, 0, 1)
                nc.vector.tensor_scalar(wide_f, bank[6][0:1, 2 * NE:3 * NE], float(CAP), None, ALU.is_gt
                                        ).then_inc(wide_ready, 1)
                v.wait_ge(wide_ready, 1)
                nc.vector.tensor_copy(wide[:, :], wide_f).then_inc(wide_ready, 1)
                v.wait_ge(more_ready, 1)
                v.wait_ge(rank_done, 1)
                nc.vector.tensor_scalar(place, iota_e[0:MORE, 0:LIST], bank[7][0:MORE, 1:2], need, ALU.is_equal, ALU.mult
                                        ).then_inc(more_ready, 1)
                v.wait_ge(list_done, 1)
                nc.vector.tensor_copy(more[:, :], bank[6][0:1, 3 * NE:3 * NE + LIST + 1])


        with nc.Block() as block:
            @block.sync
            def _(sp):
                def load(e, q, c):
                    back = ES - CPE
                    sp.wait_ge(*(expert_used(e - 1, c - back) if c >= back else expert_used(e - 2, c - back + CPE)))
                    load_expert(sp, e, q, c)

                for e in range(1, UNROLL):
                    for c in range(ES - CPE if e == 1 else 0, CPE):
                        load(e, e, c)
                with sp.Fori(1, NE // UNROLL) as i:
                    for q in range(UNROLL):
                        for c in range(CPE):
                            load(i * UNROLL + q, q, c)
                for j in range(4):
                    sp.wait_ge(*expert_used(NE - 2, CPE - 4 + j))
                    sp.dma_start(expert_w(0, j).rearrange("p (k c) -> p k c", k=KD),
                                 w_pg[:, j * 256:(j + 1) * 256].rearrange("(k p) c -> p k c", p=P)
                                 ).then_inc(e_in[j], 16)
                n_more = sp.value_load(more[0:1, LIST:LIST + 1], min_val=0, max_val=LIST)
                with sp.If(n_more > 0):
                    with sp.Fori(0, n_more) as r:
                        e = sp.value_load(more[0:1, bass.ds(r, 1)], min_val=0, max_val=NE - 1)
                        for c in range(CPE):
                            sp.wait_ge(*expert_used(r + (NE - 1), c))
                            load_expert(sp, e, UNROLL - 1, c)

            @block.gpsimd
            def _(g):
                g.memset(ysb, 0.0).then_inc(first_zero, 1)
                g.memset(G2[:, 1, :], 0.0).then_inc(first_zero, 1)
                g.wait_ge(first_zero, 2)
                g.dma_start(ysb[0:NE, :], b_dn).then_inc(first_rows, 16)
                g.wait_ge(first_rows, 16)
                g.sem_inc(y_half, 1)
                g.sem_inc(y_sb_out, 1)

            @block.tensor
            def _(pe):
                def combine_all(e, q):
                    for n, j in enumerate(ROW_ORDER):
                        if n % 2 == 0:
                            pe.wait_ge(y_half if n == 0 else y_sb_out, e + 1)
                        combine(pe, q, j).then_inc(comb_done, 1)

                def first_half(e, q, chunk, wide_e):
                    with pe.If(wide_e > 0):
                        pe.wait_ge(selw_ready, e + 1)
                        gather_wide(pe).then_inc(gathw_done, 1)
                        pe.wait_ge(xtw_ready, e + 1)
                    with pe.Else():
                        pe.sem_inc(gathw_done, 1)
                    for t in range(NT):
                        mm = pe.transpose(bank[4][:, t * P:(t + 1) * P],
                                          selg[:, q % 2, t, :, :].rearrange("p h c -> p (h c)"), ident)
                    mm.then_inc(sgt_done, 1)
                    pe.wait_ge(acc_out, e * 4 + 4)
                    with pe.If(wide_e > 0):
                        gate_up_wide(pe, chunk)
                    with pe.Else():
                        gate_up(pe, chunk, q % 2)
                    pe.wait_ge(g2_out, e + 2)
                    for hh in range(2):
                        pe.wait_ge(h_out, e * 4 + (2 + 2 * hh))
                        turn(pe, hh).then_inc(t_done, 1)

                def rows_in(e, q):
                    combine_all(e, 1 - q % 2)

                def second_half(e, chunk, product=down):
                    pe.wait_ge(t_read, e * 2 + 2)
                    for f in range(0, 8, 2):
                        if f % 4 == 0:
                            pe.wait_ge(act_ready, e * 2 + (f // 4 + 1))
                        product(pe, chunk(KD + f // 2), f)

                for t in range(NT):
                    mm = pe.transpose(bank[6][0:NE, t * P:(t + 1) * P], gate[:, t, 0:NE], ident)
                mm.then_inc(gT_done, 1)
                with pe.Fori(0, NE // UNROLL) as i:
                    for q in range(UNROLL):
                        e = i * UNROLL + q
                        pair = i * (UNROLL // 2) + q // 2
                        if q % 2 == 0:
                            pe.wait_ge(xt_ready, pair + 1)
                            pe.wait_ge(selg_ready, pair + 1)

                        def chunk(c):
                            pe.wait_ge(*expert_in(i, q, c))
                            return expert_w(q, c)

                        wide_e = pe.value_load(wide[0:1, bass.ds(e, 1)], min_val=0, max_val=1)
                        first_half(e, q, chunk, wide_e)
                        rows_in(e, q)
                        if q % 2 == 1:
                            pe.wait_ge(selg_ready, pair + 2)
                            pe.wait_ge(t_read, e * 2 + 1)
                            if q < UNROLL - 1:
                                gather(pe).then_inc(gath_done, 1)
                            else:
                                with pe.If(i < NE // UNROLL - 1):
                                    gather(pe).then_inc(gath_done, 1)
                                with pe.Else():
                                    pe.sem_inc(gath_done, 1)
                        with pe.If(wide_e > 0):
                            second_half(e, chunk, down_wide)
                        with pe.Else():
                            second_half(e, chunk)
                n_more = pe.value_load(more[0:1, LIST:LIST + 1], min_val=0, max_val=LIST)
                with pe.If(n_more > 0):
                    with pe.Fori(0, n_more) as r:
                        e = r + NE

                        def chunk(c):
                            i = (UNROLL - 1) * CPE + c
                            pe.wait_ge(e_in[i % ES], r * 16 + (16 * NE * CPE // ES + 16))
                            return expert_w(UNROLL - 1, c)

                        pe.wait_ge(h_out, e * 4)
                        pe.wait_ge(acc_out, e * 4 + 4)
                        combine_all(e, 1)
                        pe.wait_ge(selg_ready, r + (NE // 2 + 2))
                        pe.wait_ge(xt_ready, r + (NE // 2 + 1))
                        gather(pe).then_inc(gath_done, 1)
                        pe.wait_ge(xt_ready, r + (NE // 2 + 2))
                        for t in range(NT):
                            mm = pe.transpose(bank[4][:, t * P:(t + 1) * P],
                                              selg[:, 0, t, :, :].rearrange("p h c -> p (h c)"), ident)
                        mm.then_inc(sgt_done, 1)
                        pe.wait_ge(acc_out, e * 4 + 8)
                        gate_up(pe, chunk, 0)
                        pe.wait_ge(g2_out, e + 2)
                        for hh in range(2):
                            pe.wait_ge(h_out, e * 4 + (2 + 2 * hh))
                            turn(pe, hh).then_inc(t_done, 1)
                        second_half(e, chunk)
                with pe.If(n_more > 0):
                    pe.wait_ge(acc_out, n_more * 4 + (4 * NE + 4))
                    combine_all(n_more + NE, 1)
                with pe.Else():
                    pe.wait_ge(acc_out, 4 * NE + 4)
                    combine_all(NE, 1)

            @block.scalar
            def _(a):
                def gates_out(e, q):
                    a.wait_ge(sgt_done, e + 1)
                    a.activation(G2[:, q, :], bank[4][:, 0:S], ACT.Identity).then_inc(g2_out, 1)

                def sums_out(e):
                    for n, b in enumerate(BANK_ORDER):
                        a.wait_ge(gu_done, e * 4 + (n + 1))
                        a.activation(hsb[:, b * 512:(b + 1) * 512], bank[b][:, :], ACT.Identity).then_inc(h_out, 1)

                def sigmoids_wide(e):
                    for hh in range(2):
                        a.wait_ge(sig_in, e * 2 + (hh + 1))
                        a.activation(sg_w, gt_w, ACT.Sigmoid, scale=SW_ALPHA).then_inc(sig_out, 1)

                def sigmoids(e):
                    for hh in range(2):
                        a.wait_ge(sig_in, e * 2 + (hh + 1))
                        a.activation(sg[:, 4 * hh:4 * hh + 4, :], gt[:, 4 * hh:4 * hh + 4, :], ACT.Sigmoid,
                                     scale=SW_ALPHA).then_inc(sig_out, 1)

                def rows_out(e):
                    for n in range(2):
                        a.wait_ge(d_half if n == 0 else d_done, e + 1)
                        a.activation(ysb[:, n * 512:(n + 1) * 512], bank[6 + n][:, :], ACT.Identity
                                     ).then_inc(y_half if n == 0 else y_sb_out, 1)

                a.wait_ge(gT_done, 1)
                a.wait_ge(first_zero, 2)
                a.activation(G2[0:NE, 1, :], bank[6][0:NE, 0:S], ACT.Identity).then_inc(g2_out, 1)
                with a.Fori(0, NE // UNROLL) as i:
                    for q in range(UNROLL):
                        e = i * UNROLL + q
                        wide_e = a.value_load(wide[0:1, bass.ds(e, 1)], min_val=0, max_val=1)
                        with a.If(wide_e > 0):
                            a.wait_ge(gathw_done, e + 1)
                            for b in range(2):
                                a.activation(XT_w[:, 4 * b:4 * b + 4, :], bank[4 + b][:, :].rearrange("p (k c) -> p k c", k=4),
                                             ACT.Identity).then_inc(xt_half if b == 0 else xtw_ready, 1)
                        with a.Else():
                            a.sem_inc(xtw_ready, 1)
                        gates_out(e, q % 2)
                        sums_out(e)
                        with a.If(wide_e > 0):
                            sigmoids_wide(e)
                        with a.Else():
                            sigmoids(e)
                        if q % 2 == 1:
                            xt_out(a, i * (UNROLL // 2) + (q // 2 + 2))
                        rows_out(e)
                n_more = a.value_load(more[0:1, LIST:LIST + 1], min_val=0, max_val=LIST)
                with a.If(n_more > 0):
                    with a.Fori(0, n_more) as r:
                        xt_out(a, r + (NE // 2 + 2))
                        gates_out(r + NE, 1)
                        sums_out(r + NE)
                        sigmoids(r + NE)
                        rows_out(r + NE)

            @block.vector
            def _(v):
                def add_rows(n):
                    for i, j in enumerate(ROW_ORDER):
                        v.wait_ge(comb_done, n + (i + 1))
                        v.wait_ge(acc_out, n + (i + 1))
                        nc.vector.tensor_tensor(acc_part(j), bank[j][:, :], acc_part(j), ALU.add).then_inc(acc_out, 1)

                for j in ROW_ORDER:
                    nc.vector.tensor_scalar(acc_part(j), x1[:, j // 2, (j % 2) * 512:(j % 2) * 512 + 512], ALPHA,
                                            None, ALU.mult).then_inc(acc_out, 1)
                with v.Fori(0, NE // UNROLL) as i:
                    for q in range(UNROLL):
                        e = i * UNROLL + q
                        wide_e = v.value_load(wide[0:1, bass.ds(e, 1)], min_val=0, max_val=1)
                        with v.If(wide_e > 0):
                            v.wait_ge(gath_done, i * (UNROLL // 2) + (q // 2 + 1))
                            select_wide(v, e, q % 2)
                        with v.Else():
                            nc.vector.sem_inc(selw_onehot, 1)
                            nc.vector.sem_inc(slot_moved, 1)
                            nc.vector.sem_inc(selw_ready, 1)
                        if q % 2 == 1:
                            v.wait_ge(sgt_done, e + 1)
                            select(v, e + 1, i * (UNROLL // 2) + (q // 2 + 2))
                        with v.If(wide_e > 0):
                            for hh in range(2):
                                swiglu_wide(v, e, hh, e * 2 + (hh + 1))
                        with v.Else():
                            for hh in range(2):
                                swiglu(v, e, hh, e * 2 + (hh + 1))
                        add_rows(e * 4)
                n_more = v.value_load(more[0:1, LIST:LIST + 1], min_val=0, max_val=LIST)
                with v.If(n_more > 0):
                    with v.Fori(0, n_more) as r:
                        e = v.value_load(more[0:1, bass.ds(r, 1)], min_val=0, max_val=NE - 1)
                        v.wait_ge(gath_done, r + (NE // 2 + 1))
                        v.wait_ge(slot_moved, r + NE)
                        nc.vector.tensor_scalar(slot1[:, :, bass.ds(e, 1)], slot1[:, :, bass.ds(e, 1)], float(CAP),
                                                None, ALU.subtract).then_inc(slot_moved, 1)
                        v.wait_ge(slot_moved, r + (NE + 1))
                        select(v, e, r + (NE // 2 + 2))
                        add_rows(r * 4 + 4 * NE)
                        for hh in range(2):
                            swiglu(v, e, hh, r * 2 + (2 * NE + hh + 1))
                with v.If(n_more > 0):
                    add_rows(n_more * 4 + 4 * NE)
                with v.Else():
                    add_rows(4 * NE)

        def gate_bank(n):
            return bank[(4 + n) % 8][:, 0:256]

        with nc.Block() as block:
            @block.tensor
            def _(pe):
                for t in range(NT):
                    for k in range(KD):
                        mm = pe.transpose(bank[2 * t + k // 4][:, (k % 4) * P:(k % 4 + 1) * P],
                                          acc[:, t, k * P:(k + 1) * P], ident)
                        if k % 4 == 3:
                            mm.then_inc(hT_done, 1)
                for n in range(4 * NT):
                    t, j = n // 4, n % 4
                    if n == 0:
                        pe.wait_ge(hT_out, 2)
                    if n == 4:
                        pe.wait_ge(hT_out, 4)
                    if t == 0:
                        pe.wait_ge(e_in[j], 16 * (NE * CPE // ES + 1))
                    w = expert_w(0, j).rearrange("p (k c) -> p k c", k=KD)
                    for k in range(KD):
                        mm = pe.matmul(gate_bank(n), hT[:, k, t * P:(t + 1) * P], w[:, k, :],
                                       start=(k == 0), stop=(k == KD - 1))
                    mm.then_inc(pg_done, 1)

            @block.scalar
            def _(a):
                a.dma_start(lng2, ln2g.partition_broadcast(P)).then_inc(ln_in, 16)
                a.dma_start(lnb2, ln2b.partition_broadcast(P)).then_inc(ln_in, 16)
                for n in range(4):
                    a.wait_ge(hT_done, n + 1)
                    a.activation(hT[:, 4 * (n % 2):4 * (n % 2) + 4, (n // 2) * P:(n // 2 + 1) * P],
                                 bank[n][:, :].rearrange("p (k t) -> p k t", k=4), ACT.Identity).then_inc(hT_out, 1)
                for t in range(NT):
                    for j in range(4):
                        n = 4 * t + j
                        a.wait_ge(pg_done, n + 1)
                        a.activation(pge[:, t, j * 256:(j + 1) * 256], gate_bank(n), ACT.Sigmoid).then_inc(pge_ready, 1)
                    a.wait_ge(var2, t + 1)
                    a.activation(rstd[:, t:t + 1], mv[:, t, 1:2], ACT.Sqrt, bias=epsc).then_inc(std2, 1)

            @block.vector
            def _(v):
                c = Tally()
                for t in range(NT):
                    for j in range(4):
                        at = slice(j * 256, (j + 1) * 256)
                        v.wait_ge(pge_ready, 4 * t + j + 1)
                        nc.vector.tensor_tensor(pge[:, t, at], pge[:, t, at], pple[:, t, at], ALU.mult).then_inc(t_chain, 1)
                        v.wait_ge(t_chain, c.up())
                        nc.vector.tensor_tensor(pge[:, t, at], pge[:, t, at], acc[:, t, at], ALU.add).then_inc(t_chain, 1)
                        v.wait_ge(t_chain, c.up())
                        nc.vector.bn_stats(stats4[:, t, j, :], pge[:, t, at]).then_inc(t_chain, 1)
                        c.up()
                    v.wait_ge(t_chain, c.n)
                    nc.vector.bn_aggr(mv[:, t, :], stats4[:, t, :, :]).then_inc(var2, 1)
                    v.wait_ge(var2, t + 1)
                    v.wait_ge(ln_in, 64)
                    for j in range(2):
                        at = slice(j * 512, (j + 1) * 512)
                        nc.vector.scalar_tensor_tensor(pge[:, t, at], pge[:, t, at], mv[:, t, 0:1], lng2[:, at],
                                                       ALU.subtract, ALU.mult).then_inc(t_chain, 1)
                        if j == 0:
                            v.wait_ge(std2, t + 1)
                            nc.vector.reciprocal(rstd[:, t:t + 1], rstd[:, t:t + 1]).then_inc(t_chain, 1)
                            c.up()
                        v.wait_ge(t_chain, c.up())
                        nc.vector.scalar_tensor_tensor(pge[:, t, at], pge[:, t, at], rstd[:, t:t + 1], lnb2[:, at],
                                                       ALU.mult, ALU.add).then_inc(out_ready, 1)

            @block.sync
            def _(sp):
                for n in range(2 * NT):
                    t, at = n // 2, slice((n % 2) * 512, (n % 2 + 1) * 512)
                    sp.wait_ge(out_ready, n + 1)
                    sp.dma_start(out[t * P:(t + 1) * P, at], pge[:, t, at]).then_inc(out_done, 16)
                sp.wait_ge(out_done, 16 * 2 * NT)


_INS = ["x", "xT", "pT", "w_in", "bT", "bki", "b_in", "w_oa", "w_oc", "w_out", "dwT", "convT", "ln1g", "ln1b", "w_r",
        "b_r", "w_gu", "bguT", "w_dn", "b_dn", "w_pg", "w_pp", "ln2g", "ln2b", "relb", "onehot", "passes"]


def kernel(x, p, w_in, b_in, w_o_attn, w_dw, b_dw, conv_ln_g, conv_ln_b, w_o_conv, w_out, ln1_g, ln1_b,
           w_router, b_router, w_gate_up, b_gate_up, w_down, b_down, w_ple_gate, w_ple_proj, ln2_g, ln2_b, rel_bias):
    import numpy as _np
    import concourse.bacc as _bacc
    from concourse import mybir as _mybir
    from concourse.bass_utils import run_bass_kernel_spmd as _run

    def rows(a):
        return _np.asarray(a).reshape(-1, P).T

    b = _np.asarray(b_in[0])
    placed = [b[c:c + n] for c, n in ((QI0, 512), (Q0, 512), (K0, 512), (CA0, 512), (CG0, 512), (GA0, D), (GC0, D))]
    given = {
        "x": x[0], "xT": _np.asarray(x[0]).T, "pT": _np.asarray(p[0, 0]).T, "w_in": w_in[0],
        "bT": _np.concatenate([rows(a) for a in placed], axis=1),
        "bki": _np.concatenate([b[KI0:WI0], b[KI0:WI0]])[:, None], "b_in": b,
        "w_oa": w_o_attn[0], "w_oc": w_o_conv[0], "w_out": w_out[0],
        "dwT": _np.asarray(w_dw[0]).T.reshape(4, P, CW).transpose(1, 0, 2).reshape(P, 4 * CW),
        "convT": _np.concatenate([rows(a[0]) for a in (b_dw, conv_ln_g, conv_ln_b)], axis=1),
        "ln1g": ln1_g[0], "ln1b": ln1_b[0], "w_r": w_router[0], "b_r": b_router[0],
        "w_gu": w_gate_up[0], "bguT": rows(_np.asarray(b_gate_up[0]).reshape(-1)), "w_dn": w_down[0],
        "b_dn": b_down[0], "w_pg": w_ple_gate[0], "w_pp": w_ple_proj[0], "ln2g": ln2_g[0], "ln2b": ln2_b[0],
        "relb": rel_bias, "onehot": rel_bucket_onehot(),
        "passes": further_passes(),
    }
    nc = _bacc.Bacc("TRN2", target_bir_lowering=False, num_devices=1)
    arrays, args = {}, []
    for name in _INS:
        a = _np.ascontiguousarray(given[name])
        arrays[f"in_{name}"] = a
        args.append(nc.dram_tensor(f"in_{name}", a.shape, _mybir.dt.from_np(a.dtype), kind="ExternalInput").ap())
    out = nc.dram_tensor("out_0", (S, D), _mybir.dt.float32, kind="ExternalOutput").ap()
    table = nc.dram_tensor("bias_table", (H, S + P), _mybir.dt.float32, kind="Internal").ap()
    program(nc, *args, out, table)
    r = _run(nc, [arrays], core_ids=[0])
    return r.results[0]["out_0"].reshape(1, S, D)
```
